# Optimizing a Trainium2 kernel written in Bass

```python
import math
import jax, jax.numpy as jnp
from jax import lax
import numpy as np

D_MODEL = 1024
BATCH = 1
SEQ = 1024
DEPTH = 1
DEC_BATCH = 8
DEC_SEQ = 4
PAST_LEN = 2048
PAGE_SIZE = 128

HEAD_DIM = 64
N_ATT_HEADS = 8
ATT_DIM = N_ATT_HEADS * HEAD_DIM
CONV_DIM = D_MODEL - ATT_DIM
CONV_WIDTH = 3
MIX_IN = 3 * ATT_DIM + 3 * CONV_DIM
SPLITS = (ATT_DIM, 2 * ATT_DIM, 3 * ATT_DIM, 3 * ATT_DIM + CONV_DIM, 3 * ATT_DIM + 2 * CONV_DIM)
DILATED_PATTERNS = ((128, 1), (512, 4), (2048, 16))
ATT_WINDOW_MAX = 2048
Q_BLOCK = 128
N_BUCKETS = 32
MAX_DISTANCE = 2048
N_GROUPS = 4
EXPERTS_PER_GROUP = 8
N_EXPERTS = N_GROUPS * EXPERTS_PER_GROUP
TOP_K = 2
D_EXPERT = 256
D_PLE = 256
EPS = 1e-6
NEG = -1e30

kernel_name = "hybrid_dilated_attn_shortconv_hmoe_step"

def rms_norm(x, gain):
    xf = x.astype(jnp.float32)
    y = xf * lax.rsqrt(jnp.mean(xf * xf, axis=-1, keepdims=True) + EPS)
    return (y * gain.astype(jnp.float32)).astype(x.dtype)

def t5_bucket(dist):
    max_exact = N_BUCKETS // 2
    d_f = jnp.maximum(dist, 1).astype(jnp.float32)
    large = max_exact + (jnp.log(d_f / max_exact) / math.log(MAX_DISTANCE / max_exact)
                         * (N_BUCKETS - max_exact)).astype(jnp.int32)
    large = jnp.minimum(large, N_BUCKETS - 1)
    return jnp.where(dist < max_exact, dist, large)

def pattern_bias(rel_bias, dilation, n_k):
    dist = dilation * jnp.arange(n_k + 1, dtype=jnp.int32)
    return rel_bias[t5_bucket(dist)]

def band_pattern_stats(q, k, v, rel_bias, window, dilation):
    B, S, H, Dh = q.shape
    n_k = window // dilation
    M = S // dilation
    nb = -(-M // Q_BLOCK)
    Mp = nb * Q_BLOCK

    def split(t):
        return jnp.swapaxes(t.reshape(B, M, dilation, H, Dh), 1, 2)

    qs, ks, vs = split(q), split(k), split(v)
    qb = jnp.pad(qs, ((0, 0), (0, 0), (0, Mp - M), (0, 0), (0, 0))).reshape(B, dilation, nb, Q_BLOCK, H, Dh)

    def band(t):
        tp = jnp.pad(t, ((0, 0), (0, 0), (Q_BLOCK, Mp - M), (0, 0), (0, 0)))
        prev = tp[:, :, :Mp].reshape(B, dilation, nb, Q_BLOCK, H, Dh)
        cur = tp[:, :, Q_BLOCK:].reshape(B, dilation, nb, Q_BLOCK, H, Dh)
        return jnp.concatenate([prev, cur], axis=3)

    kb, vb = band(ks), band(vs)
    i = jnp.arange(Q_BLOCK)[:, None]
    j = jnp.arange(2 * Q_BLOCK)[None, :]
    off = i - j + Q_BLOCK
    key_idx = jnp.arange(nb)[:, None, None] * Q_BLOCK + j[None] - Q_BLOCK
    valid = (off >= 0) & (off <= n_k) & (key_idx >= 0)
    bias = pattern_bias(rel_bias, dilation, n_k)[jnp.clip(off, 0, n_k)].transpose(2, 0, 1)

    s = jnp.einsum('bdnqhc,bdnkhc->bdnhqk', qb, kb, preferred_element_type=jnp.float32)
    s = s * (HEAD_DIM ** -0.5) + bias.astype(jnp.float32)
    s = jnp.where(valid[None, None, :, None], s, NEG)
    mx = jnp.max(s, axis=-1, keepdims=True)
    e = jnp.exp(s - mx)
    den = jnp.sum(e, axis=-1)
    num = jnp.einsum('bdnhqk,bdnkhc->bdnqhc', e, vb.astype(jnp.float32))

    def merge(t):
        rest = t.shape[4:]
        t = t.reshape((B, dilation, Mp) + rest)[:, :, :M]
        return jnp.swapaxes(t, 1, 2).reshape((B, S) + rest)

    mx = jnp.swapaxes(mx[..., 0], 3, 4)
    den = jnp.swapaxes(den, 3, 4)
    return merge(num), merge(mx), merge(den)

def dilated_attention_prompt(q, k, v, rel_bias):
    stats = [band_pattern_stats(q, k, v, rel_bias, w, d) for (w, d) in DILATED_PATTERNS]
    nums = jnp.stack([st[0] for st in stats])
    mxs = jnp.stack([st[1] for st in stats])
    dens = jnp.stack([st[2] for st in stats])
    wts = jnp.exp(mxs - jnp.max(mxs, axis=0))
    num = jnp.einsum('pbsh,pbshc->bshc', wts, nums)
    den = jnp.sum(wts * dens, axis=0)
    return num / den[..., None]

def dilated_attention_sample(q, k_all, v_all, rel_bias):
    T = q.shape[1]
    L = k_all.shape[1]
    q_idx = L - T + jnp.arange(T, dtype=jnp.int32)
    idxs, biases = [], []
    for (w, d) in DILATED_PATTERNS:
        n_k = w // d
        dist = d * jnp.arange(n_k + 1, dtype=jnp.int32)
        idxs.append(q_idx[:, None] - dist[None, :])
        biases.append(pattern_bias(rel_bias, d, n_k))
    idx = jnp.concatenate(idxs, axis=1)
    bias = jnp.concatenate(biases, axis=0)
    valid = idx >= 0
    idx = jnp.clip(idx, 0, L - 1)
    kg = k_all[:, idx]
    vg = v_all[:, idx]
    s = jnp.einsum('bthc,btkhc->bthk', q, kg, preferred_element_type=jnp.float32)
    s = s * (HEAD_DIM ** -0.5) + bias.T.astype(jnp.float32)[None, None]
    s = jnp.where(valid[None, :, None, :], s, NEG)
    p = jax.nn.softmax(s, axis=-1)
    return jnp.einsum('bthk,btkhc->bthc', p, vg.astype(jnp.float32))

def token_mixers(a, rel_bias, w_in, q_gain, k_gain, conv_w, g_out_att, g_out_conv, w_out,
                 k_past, v_past, conv_past):
    B, T, _ = a.shape
    proj = jnp.einsum('btd,dm->btm', a, w_in)
    q, k, v, hc, gb, gc = jnp.split(proj, SPLITS, axis=-1)
    q = rms_norm(q.reshape(B, T, N_ATT_HEADS, HEAD_DIM), q_gain)
    k = rms_norm(k.reshape(B, T, N_ATT_HEADS, HEAD_DIM), k_gain)
    v = v.reshape(B, T, N_ATT_HEADS, HEAD_DIM)
    if k_past is None:
        att = dilated_attention_prompt(q, k, v, rel_bias)
        keep = min(ATT_WINDOW_MAX, T)
        new_k, new_v = k[:, T - keep:], v[:, T - keep:]
        u_prev = jnp.zeros((B, CONV_WIDTH - 1, CONV_DIM), a.dtype)
    else:
        att = dilated_attention_sample(q, jnp.concatenate([k_past.astype(k.dtype), k], axis=1),
                                       jnp.concatenate([v_past.astype(v.dtype), v], axis=1), rel_bias)
        new_k, new_v = k, v
        u_prev = conv_past.astype(a.dtype)
    u = gc * hc
    u_ext = jnp.concatenate([u_prev, u], axis=1)
    conv = conv_w[0] * u_ext[:, 0:T]
    for j in range(1, CONV_WIDTH):
        conv = conv + conv_w[j] * u_ext[:, j:j + T]
    y_conv = gb * conv
    new_conv = u_ext[:, -(CONV_WIDTH - 1):]
    merged = jnp.concatenate([rms_norm(att.astype(a.dtype).reshape(B, T, ATT_DIM), g_out_att),
                              rms_norm(y_conv, g_out_conv)], axis=-1)
    return jnp.einsum('btm,md->btd', merged, w_out), new_k, new_v, new_conv

def hier_moe(m, w_router_group, w_router_expert, w_gate, w_up, w_down):
    B, T, _ = m.shape
    g_logits = jnp.einsum('btd,dg->btg', m, w_router_group, preferred_element_type=jnp.float32)
    g_prob = jax.nn.softmax(g_logits, axis=-1)
    g_w, g_sel = lax.top_k(g_prob, 1)
    e_logits = jnp.einsum('btd,de->bte', m, w_router_expert, preferred_element_type=jnp.float32)
    e_logits = e_logits.reshape(B, T, N_GROUPS, EXPERTS_PER_GROUP)
    e_logits = jnp.take_along_axis(e_logits, g_sel[..., None], axis=2)[:, :, 0]
    top_v, top_i = lax.top_k(e_logits, TOP_K)
    w_k = jax.nn.softmax(top_v, axis=-1) * g_w
    expert_id = g_sel * EXPERTS_PER_GROUP + top_i
    gates = jnp.einsum('btk,btke->bte', w_k, jax.nn.one_hot(expert_id, N_EXPERTS, dtype=jnp.float32))
    hg = jnp.einsum('btd,edf->btef', m, w_gate)
    hu = jnp.einsum('btd,edf->btef', m, w_up)
    hidden = jax.nn.silu(hg) * hu * gates[..., None].astype(m.dtype)
    return jnp.einsum('btef,efd->btd', hidden, w_down)

def decoder_layer(h, p_i, k_past, v_past, conv_past, g_mix, g_ffn, mix_w, ffn_w, ple_w):
    mixed, new_k, new_v, new_conv = token_mixers(rms_norm(h, g_mix), *mix_w, k_past, v_past, conv_past)
    h = h + mixed
    h = h + hier_moe(rms_norm(h, g_ffn), *ffn_w)
    g_ple, w_ple_gate, w_ple_proj = ple_w
    gate = jax.nn.sigmoid(jnp.einsum('btd,de->bte', rms_norm(h, g_ple), w_ple_gate))
    h = h + jnp.einsum('btp,pd->btd', p_i, w_ple_proj) * gate
    return h, new_k, new_v, new_conv

def setup_inputs(seed: int = 0) -> dict:
    key = jax.random.key(seed)
    ks = jax.random.split(key, 26)
    f32 = jnp.float32
    w_buf = min(ATT_WINDOW_MAX, PAST_LEN)

    def nrm(k, shape, scale):
        return scale * jax.random.normal(k, shape, f32)

    def gain(k, shape):
        return 1.0 + 0.1 * jax.random.normal(k, shape, f32)

    return {
        "x_prompt": nrm(ks[0], (BATCH, SEQ, D_MODEL), 1.0),
        "x_sample": nrm(ks[1], (DEC_BATCH, DEC_SEQ, D_MODEL), 1.0),
        "cache_k": nrm(ks[2], (DEPTH, DEC_BATCH, w_buf, N_ATT_HEADS, HEAD_DIM), 1.0),
        "cache_v": nrm(ks[3], (DEPTH, DEC_BATCH, w_buf, N_ATT_HEADS, HEAD_DIM), 1.0),
        "state_conv": nrm(ks[4], (DEPTH, DEC_BATCH, CONV_WIDTH - 1, CONV_DIM), 1.0),
        "p_prompt": nrm(ks[5], (DEPTH, BATCH, SEQ, D_PLE), 1.0),
        "p_sample": nrm(ks[6], (DEPTH, DEC_BATCH, DEC_SEQ, D_PLE), 1.0),
        "rel_bias": nrm(ks[7], (N_BUCKETS, N_ATT_HEADS), 0.5),
        "g_mix": gain(ks[8], (DEPTH, D_MODEL)),
        "w_in": nrm(ks[9], (DEPTH, D_MODEL, MIX_IN), D_MODEL ** -0.5),
        "q_gain": gain(ks[10], (DEPTH, HEAD_DIM)),
        "k_gain": gain(ks[11], (DEPTH, HEAD_DIM)),
        "conv_w": nrm(ks[12], (DEPTH, CONV_WIDTH, CONV_DIM), CONV_WIDTH ** -0.5),
        "g_out_att": gain(ks[13], (DEPTH, ATT_DIM)),
        "g_out_conv": gain(ks[14], (DEPTH, CONV_DIM)),
        "w_out": nrm(ks[15], (DEPTH, D_MODEL, D_MODEL), D_MODEL ** -0.5),
        "g_ffn": gain(ks[16], (DEPTH, D_MODEL)),
        "w_router_group": nrm(ks[17], (DEPTH, D_MODEL, N_GROUPS), D_MODEL ** -0.5),
        "w_router_expert": nrm(ks[18], (DEPTH, D_MODEL, N_EXPERTS), D_MODEL ** -0.5),
        "w_gate": nrm(ks[19], (DEPTH, N_EXPERTS, D_MODEL, D_EXPERT), D_MODEL ** -0.5),
        "w_up": nrm(ks[20], (DEPTH, N_EXPERTS, D_MODEL, D_EXPERT), D_MODEL ** -0.5),
        "w_down": nrm(ks[21], (DEPTH, N_EXPERTS, D_EXPERT, D_MODEL), D_EXPERT ** -0.5),
        "g_ple": gain(ks[22], (DEPTH, D_MODEL)),
        "w_ple_gate": nrm(ks[23], (DEPTH, D_MODEL, D_MODEL), D_MODEL ** -0.5),
        "w_ple_proj": nrm(ks[24], (DEPTH, D_PLE, D_MODEL), D_PLE ** -0.5),
    }

def reference(x_prompt, x_sample, cache_k, cache_v, state_conv, p_prompt, p_sample,
              rel_bias, g_mix, w_in, q_gain, k_gain, conv_w, g_out_att, g_out_conv, w_out,
              g_ffn, w_router_group, w_router_expert, w_gate, w_up, w_down,
              g_ple, w_ple_gate, w_ple_proj):
    hp, hs = x_prompt, x_sample
    kp_l, vp_l, cp_l, ks_l, vs_l, cs_l = [], [], [], [], [], []
    for i in range(DEPTH):
        mix_w = (rel_bias, w_in[i], q_gain[i], k_gain[i], conv_w[i], g_out_att[i], g_out_conv[i], w_out[i])
        ffn_w = (w_router_group[i], w_router_expert[i], w_gate[i], w_up[i], w_down[i])
        ple_w = (g_ple[i], w_ple_gate[i], w_ple_proj[i])
        hp, kp, vp, cp = decoder_layer(hp, p_prompt[i], None, None, None, g_mix[i], g_ffn[i],
                                       mix_w, ffn_w, ple_w)
        hs, ksn, vsn, csn = decoder_layer(hs, p_sample[i], cache_k[i], cache_v[i], state_conv[i],
                                          g_mix[i], g_ffn[i], mix_w, ffn_w, ple_w)
        kp_l.append(kp); vp_l.append(vp); cp_l.append(cp)
        ks_l.append(ksn); vs_l.append(vsn); cs_l.append(csn)
    new_k_prompt = jnp.stack(kp_l)
    new_v_prompt = jnp.stack(vp_l)
    new_conv_prompt = jnp.stack(cp_l)
    new_k_sample = jnp.stack(ks_l)
    new_v_sample = jnp.stack(vs_l)
    new_conv_sample = jnp.stack(cs_l)
    return (hp, hs, new_k_prompt, new_v_prompt, new_conv_prompt, new_k_sample, new_v_sample, new_conv_sample)


_drawn_inputs = setup_inputs


def setup_inputs(seed=0):
    import zlib

    import numpy as np

    out = dict(_drawn_inputs(seed))
    spreads = {}
    factors = {'g_ple': 4.103}
    for name, (base, spread) in spreads.items():
        noise = np.random.default_rng([zlib.crc32(name.encode()), seed]).standard_normal(out[name].shape)
        drawn = base * np.exp(spread * noise) if base else spread * noise
        out[name] = __import__('jax').numpy.asarray(drawn.astype(out[name].dtype))
    for name, factor in factors.items():
        out[name] = (out[name] * factor).astype(out[name].dtype)
    return out
```

```python
import math
from contextlib import ExitStack

import numpy as np
import concourse.bass as bass
from concourse import mybir

F32 = mybir.dt.float32
I32 = mybir.dt.int32
BF16 = mybir.dt.bfloat16
ALU = mybir.AluOpType
ACT = mybir.ActivationFunctionType
AX = mybir.AxisListType

P = 128
D = 1024
SEQ = 1024
NB, NT = 8, 4
SAMP = NB * NT
PT = SEQ // P
TILES = PT + 1
TOK = SEQ + SAMP
H, DH = 8, 64
AD = H * DH
CD = D - AD
MIX = 3 * AD + 3 * CD
PAST = 2048
DC = D // P
CC = CD // P
NG = 4
PATTERNS = ((128, 1), (512, 4), (2048, 16))
NBUCKET, MAXD = 32, 2048
GROUPS, EPG = 4, 8
NE = GROUPS * EPG
FE = 256
PLE = 256
EPS = 1e-6
NEG = -1e30
NEAR, FAR = 512, 96
SK = NEAR + NT * FAR
SKN = SK + SAMP
CAP = 128
NOV = 16
NBLK = NE + NOV
NTH = -(-TOK // CAP)
ZLEN = 1152
RG = GROUPS + NE


def bucket(dist):
    dist = np.maximum(dist, 0)
    half = NBUCKET // 2
    large = half + (np.log(np.maximum(dist, 1) / half) / math.log(MAXD / half) * (NBUCKET - half)).astype(np.int64)
    return np.where(dist < half, dist, np.minimum(large, NBUCKET - 1))


def log_count(dist):
    n = sum(((dist >= 0) & (dist <= w) & (dist % d == 0)).astype(np.int64) for w, d in PATTERNS)
    return np.where(n > 0, np.log(np.maximum(n, 1)), NEG).astype(np.float32)


def constants():
    c = {}
    c["c_ident"] = np.eye(P, dtype=np.float32)
    k = np.arange(P)
    c["c_tri"] = (k[:, None] < k[None, :]).astype(np.float32)
    dist = SEQ - 1 - np.arange(ZLEN)
    c["c_hot_p"] = (bucket(dist)[None, :] == np.arange(NBUCKET)[:, None]).astype(np.float32)
    c["c_log_p"] = np.tile(log_count(dist)[None, :], (H, 1))
    row = np.zeros(SK, np.int64)
    col = np.arange(NEAR)
    row[:NEAR] = PAST - NEAR + 4 * (col % P) + col // P
    col = np.arange(NT * FAR)
    row[NEAR:] = 16 * (col % FAR) + col // FAR
    t = np.arange(NT)
    cache_dist = PAST + t[:, None] - row[None, :]
    new_t = np.arange(SAMP) % NT
    new_dist = t[:, None] - new_t[None, :]
    dist_s = np.concatenate([cache_dist, new_dist, new_dist], 1)
    hot = bucket(dist_s)[:, None, :] == np.arange(NBUCKET)[None, :, None]
    c["c_hot_s"] = hot.reshape(P, SK + 2 * SAMP).astype(np.float32)
    log = np.zeros((4, NT, H, SK + 2 * SAMP), np.float32)
    log[:] = log_count(dist_s)[None, :, None, :]
    for bb in range(4):
        for grp in range(2):
            other = np.arange(SAMP) // NT != 4 * grp + bb
            log[bb, :, :, SK + SAMP * grp:SK + SAMP * (grp + 1)][:, :, other] = NEG
    c["c_log_s"] = log.reshape(P, -1)
    r = np.arange(P)
    c["c_mask"] = (r[:, None] % H == np.arange(AD)[None, :] // DH).astype(np.float32)
    c["c_sel"] = np.stack([(np.arange(SAMP)[None, :] == 16 * g + r[:, None] // H) for g in range(2)], 1).astype(np.float32)
    misc = np.zeros((P, 64), np.float32)
    misc[:, 0:NE] = np.arange(NE)
    misc[:, NE:NE + NTH - 1] = CAP * np.arange(1, NTH)
    misc[:SAMP, 63] = 1.0
    c["c_misc"] = misc
    tok = (P * np.arange(TILES)[None, :] + r[:, None])
    code = np.stack([np.stack([tok, kk * TOK + tok], -1) for kk in range(2)], 2)
    c["c_code"] = code.astype(np.int32).reshape(P, TILES * 4)
    c["c_blk"] = np.tile(np.arange(NOV, dtype=np.float32)[None, :], (P, 1))
    return c


class Tile:

    def __init__(self, t, u, k, rows=P):
        self.t, self.u, self.k, self.rows = t, u, k, rows
        self.first = isinstance(t, int) and t == 0
        self.early = isinstance(t, int) and t < 2


T = TILES
USES = ((TILES + 1) // 2, TILES // 2)


ORDER = [(hh, i) for i in range(PT) for hh in range(2)]


def tp_uses(n):
    return sum(-(-(i + 1) // 4) for _, i in ORDER[:n])


def fixed(t):
    return Tile(t, t % 2, t // 2, P if t < PT else SAMP)


def over_tiles(eng, step):
    step(None, fixed(0), fixed(1))
    with eng.Fori(0, 3) as i:
        step(Tile(2 * i, 0, i), Tile(2 * i + 1, 1, i), Tile(2 * i + 2, 0, i + 1))
        step(Tile(2 * i + 1, 1, i), Tile(2 * i + 2, 0, i + 1), Tile(2 * i + 3, 1, i + 1))
    step(fixed(6), fixed(7), fixed(8))
    step(fixed(7), fixed(8), None)


def waits_end(eng, seen):
    eng.sem_inc(seen, 1)


def rows_of(prompt, sample, a):
    return sample if a.rows == SAMP else prompt[bass.ds(a.t * P, P), :]


def build(nc, I, O):
    ctx = ExitStack()
    with ctx, nc.allow_non_contiguous_dma(reason="gains and router weights, a few KB"):
        _build(nc, I, O, ctx)


def _build(nc, I, O, ctx):
    sem_cache = {}

    def S(name):
        if name not in sem_cache:
            sem_cache[name] = ctx.enter_context(nc.semaphore(name))
        return sem_cache[name]

    def sb(name, n, dt=F32):
        return ctx.enter_context(nc.sbuf_tensor(name, [P, n], dt))

    brev = nc.dram_tensor("brev_dram", [H, ZLEN], F32).ap()
    m_dram = nc.dram_tensor("m_dram", [TOK, D], F32).ap()
    y_dram = nc.dram_tensor("y_dram", [2 * TOK, D], F32).ap()
    list_dram = nc.dram_tensor("list_dram", [CAP * NBLK, 2], I32).ap()

    def view(region, at, *dims):
        n = int(np.prod(dims))
        v = region[:, at:at + n]
        if len(dims) == 2:
            v = v.rearrange("p (a b) -> p a b", a=dims[0])
        if len(dims) == 3:
            v = v.rearrange("p (a b c) -> p a b c", a=dims[0], b=dims[1])
        return v

    ident = sb("ident", P)
    tri = sb("tri", P)
    ones = sb("ones", P)
    bias_s = sb("bias_s", SK + SAMP)
    bias_new = sb("bias_new", 2 * SAMP)
    misc = sb("misc", 64)
    gmix = sb("gmix", DC)
    gatt = sb("gatt", CC)
    gconv = sb("gconv", CC)
    convw = sb("convw", 3 * CC)
    gqk = sb("gqk", 2 * DH)
    stT = sb("stT", CC * 16)
    u_new = sb("u_new", CC * 18)
    small = sb("small", 320)
    qts = view(sb("qts", NG * SAMP), 0, NG, SAMP)
    kts = view(sb("kts", NG * SAMP), 0, NG, SAMP)
    R1 = sb("R1", 26880)
    R2 = sb("R2", 12880)
    R3 = sb("R3", 4224)
    R4 = sb("R4", 6144)

    xT = view(R1, 0, DC, TOK)
    wA = view(R1, 8448, DC, 3 * AD)
    wB = [R1[:, 20736 + 3072 * s:20736 + 3072 * (s + 1)].rearrange("p (a b c) -> p a b c", a=DC, b=3) for s in range(2)]
    QT = view(R2, 0, NG, SEQ)
    KT = view(R2, 4096, NG, SEQ)
    V = view(R2, 8192, TILES, H, DH + 1)
    yT = view(R3, 0, CC, TOK)
    x_in = [view(R3, 1024 * s, D) for s in range(2)]
    qk_sq = view(R3, 2048, D)
    junk = R3[:, 3072:3072 + 512].bitcast(BF16)
    bp = R1[0:H, 20736:20736 + ZLEN]
    logp = R4[0:H, 1152:1152 + ZLEN]
    hotp = R4[0:NBUCKET, 2304:2304 + ZLEN]
    hots = R4[:, 3456:3456 + SK + 2 * SAMP]
    relp = R4[0:NBUCKET, 4416:4424]
    relbd = R4[:, 4424:4424 + P]
    st_in = R4[0:16, 4552:4552 + CD]
    xTs = [view(R4, 1024 * s, DC, P) for s in range(2)]
    qk = [view(R4, 2048 + 1024 * s, D) for s in range(2)]
    c_sb = view(R4, 0, TOK)
    u_p = view(R4, 1056, SEQ + 2)
    u_s = view(R4, 2082, NB, NT + 2)
    conv = view(R4, 2130, TOK)
    y_sq = view(R4, 3186, TOK)
    y_sum = view(R4, 4242, TOK)
    new_out = R4[0:18, 5298:5298 + CD]
    KV = [view(R1, 4096 * s, 2, 4, AD) for s in range(3)] + [view(R1, 15872, 2, 4, AD)]
    ktc = view(R1, 12288, NG, SK)
    Z = [view(R1, 15872 + 1024 * s, SEQ) for s in range(4)]
    qst = [view(R1, 19968 + 1024 * s, SEQ) for s in range(2)]
    kst = [view(R1, 12288 + 1024 * s, SEQ) for s in range(2)]
    att = view(R1, 22016, TILES, AD)
    Eb = [view(R4, 1024 * s, SEQ) for s in range(2)]
    PTb = [view(R4, 2048 + 1024 * s, PT, P) for s in range(2)]
    Es = view(R4, 0, SKN)
    PTs = view(R4, 2048, 9, P)
    qbd = R4[:, 4096:4096 + 512].rearrange("p (b g t h) -> p b g t h", b=4, g=NG, t=NT)
    masked = view(R4, 4608, AD)
    mask = view(R4, 5136, AD)
    sel = view(R4, 5648, 2, SAMP)
    sel_st = view(R4, 5712, SAMP)
    vst = [view(r, at, PT, 2, DH + 1) for r, at in ((R1, 14336), (R4, 4096))]
    OT = [R1[0:DH + 1, 15376 + P * s:15376 + P * (s + 1)] for s in range(2)]
    w_out = view(R2, 0, 2 * CC, D)
    gffn = view(R1, 9216, D)
    gple = view(R2, 9216, D)
    w_rt = view(R1, 10240, DC, RG)
    x_re = [view(R1, 10528 + 1024 * s, D) for s in range(2)]
    m_st = [view(R1, 12576 + 1024 * s, D) for s in range(2)]
    mT = [view(R1, 14624 + 1024 * s, DC, P) for s in range(2)]
    at_st = [view(R1, 16672 + 512 * s, AD) for s in range(2)]
    y_st = [view(R1, 17696 + 512 * s, CC, P) for s in range(2)]
    atT = [view(R1, 18720 + 512 * s, CC, P) for s in range(2)]
    junkE = R1[:, 19744:19744 + 512].bitcast(BF16)
    h = view(R1, 0, TILES, D)
    scratch_at = [21504]

    def scratch(*dims):
        at = scratch_at[0]
        scratch_at[0] += int(np.prod(dims))
        assert scratch_at[0] <= 26880
        return view(R1, at, *dims)

    r_ms, r_h1, r_h2, r_t, r_tot, r_rank, r_a = (scratch(T, NE) for _ in range(7))
    r_cum = scratch(T + 1, NE)
    r_big = scratch(NE, NTH - 1)
    r_ov = scratch(4, NE)
    r_bb = scratch(NOV, NE)
    r_be = scratch(NOV)
    r_hg, r_hg2, r_ge = (scratch(T, GROUPS) for _ in range(3))
    r_c10 = scratch(T, NTH - 1)
    r_mg, r_ig, r_m1, r_i1, r_m2, r_i2, r_rk, r_bs, r_c, r_s, r_z, r_x, r_gw, r_e2 = (scratch(T) for _ in range(14))
    pos_i = sb("pos_i", 2 * TILES, I32)
    code = sb("code", 4 * TILES, I32)
    blk = sb("blk", NOV)
    ov_e = sb("ov_e", NOV, I32)
    small_i = sb("small_i", 4, I32)
    lg = sb("lg", TILES * RG)[:, :].rearrange("p (t c) -> p t c", t=TILES)
    SLOTS = [R4[:, 0:6144], R2[:, 0:6144], R1[:, 9216:15360], R1[:, 15360:21504]]
    wg = [s[:, 0:2048].rearrange("p (c f) -> p c f", c=DC) for s in SLOTS]
    wu = [s[:, 2048:4096].rearrange("p (c f) -> p c f", c=DC) for s in SLOTS]
    wd = [s[:, 4096:6144].rearrange("p (c f) -> p c f", c=2) for s in SLOTS]
    xg = [R3[0:CAP, 1024 * s:1024 * (s + 1)] for s in range(2)]
    xgT = [view(R3, 2048 + DC * CAP * s, DC, CAP) for s in range(2)]
    hT = [view(bias_s, 2 * CAP * s, 2, CAP) for s in range(2)]
    yo = [R2[0:CAP, 10240 + 1024 * s:10240 + 1024 * (s + 1)] for s in range(2)]
    sg = [view(R2, 12288 + 2 * CAP * s, 2, CAP) for s in range(2)]
    lists = sb("lists", 2 * NBLK, I32)
    idx_c = sb("idx_c", 4, I32)
    w_pg = [view(R1, 21504 + 1024 * c, D) for c in range(5)] + [view(R2, 6144 + 1024 * c, D) for c in range(3)]
    y0, y1, h2, hn = ([view(R1, 9216 + 2048 * k + 1024 * s, D) for s in range(2)] for k in range(4))
    hnT = [view(R1, 17408 + 1024 * s, DC, P) for s in range(2)]
    gs = [view(R1, 19456 + 1024 * s, D) for s in range(2)]
    ot = [view(R2, 1024 * s, D) for s in range(2)]
    w_pp = view(R2, 2048, 2, D)
    p_in = [view(R2, 4096 + 256 * s, PLE) for s in range(2)]
    pT = [view(R2, 4608 + 256 * s, 2, P) for s in range(2)]
    junkH = R2[:, 5120:5120 + 512].bitcast(BF16)
    w12 = sb("w12", 2 * TILES)[:, :].rearrange("p (k t) -> p k t", k=2)

    ssx, ms_x, rs_x = small[:, 0:2], small[:, 2:4], small[:, 4:6]
    hd_s, hd_r, hd_q = small[:, 6:22], small[:, 22:38], small[:, 38:54]
    nmax, den, rden = small[:, 54:56], small[:, 56:72], small[:, 72:88]
    ssc, rc = small[:, 88:97], small[:, 97:106]
    nms, dens, rdens = small[:, 106:107], small[:, 107:108], small[:, 108:109]
    ssa, msa, ra = small[:, 110:112], small[:, 112:114], small[:, 114:116]
    ssh, msh, rsh = small[:, 116:118], small[:, 118:120], small[:, 120:122]
    eps = small[:, 128:129]
    ssf, msf, rsf = small[:, 122:124], small[:, 124:126], small[:, 126:128]

    bank = [ctx.enter_context(nc.psum_tensor(f"pair{i}", [P, 1024], F32)) for i in range(4)]
    bk = [bank[i // 2][:, 512 * (i % 2):512 * (i % 2) + 512] for i in range(8)]

    w_in_r = I["w_in"][0].rearrange("(p c) n -> p c n", c=DC)
    w_conv_r = I["w_in"][0].rearrange("(p c) (s q m) -> p c s q m", c=DC, s=6, m=P)
    wg_r = I["w_gate"][0].rearrange("e (p c) f -> e p (c f)", c=DC)
    wu_r = I["w_up"][0].rearrange("e (p c) f -> e p (c f)", c=DC)
    wd_r = I["w_down"][0].rearrange("e (p c) f -> e p (c f)", c=2)
    xp, xs = I["x_prompt"][0], I["x_sample"].rearrange("b t d -> (b t) d")
    ck = I["cache_k"][0].rearrange("b r h d -> b r (h d)")
    cv = I["cache_v"][0].rearrange("b r h d -> b r (h d)")

    block = ctx.enter_context(nc.Block())

    NCONST = 15

    @block.sync
    def _(sp):
        def const(dst, src):
            sp.dma_start(dst, src).then_inc(S("const_in"), 16)

        const(ident[:, :], I["c_ident"])
        const(gmix[:, :], I["g_mix"][0].rearrange("(p c) -> p c", c=DC))

        def load_x(a):
            if not a.early:
                sp.wait_ge(S("xT_full"), 2 * a.t - 2)
            sp.dma_start(x_in[a.u][0:a.rows, :], rows_of(xp, xs, a)).then_inc(S(f"in{a.u}"), 16)

        load_x(fixed(0))
        const(relp, I["rel_bias"])
        const(hotp, I["c_hot_p"])
        const(logp, I["c_log_p"])
        const(hots, I["c_hot_s"])
        const(bias_s[:, 0:SK], I["c_log_s"][:, 0:SK])
        const(bias_new[:, :], I["c_log_s"][:, SK:SK + 2 * SAMP])
        const(st_in, I["state_conv"][0].rearrange("b j c -> (b j) c"))
        const(tri[:, :], I["c_tri"])
        const(misc[:, :], I["c_misc"])
        const(gatt[:, :], I["g_out_att"][0].rearrange("(c p) -> p c", p=P))
        const(gconv[:, :], I["g_out_conv"][0].rearrange("(c p) -> p c", p=P))
        const(convw[:, :].rearrange("p (j c) -> p j c", j=3), I["conv_w"][0].rearrange("j (c p) -> p j c", p=P))
        const(gqk[:, 0:DH], I["q_gain"][0:1, :].broadcast_to([P, DH]))
        sp.dma_start(code[:, :], I["c_code"]).then_inc(S("code_in"), 16)
        sp.dma_start(blk[:, :], I["c_blk"]).then_inc(S("code_in"), 16)
        sp.wait_ge(S("relbd_zero"), 1)
        for t in range(NT):
            sp.dma_start(relbd[NBUCKET * t:NBUCKET * (t + 1), :].rearrange("p (b t h) -> p b t h", b=4, t=NT)[:, :, t, :],
                         I["rel_bias"].unsqueeze(1).broadcast_to([NBUCKET, 4, H])).then_inc(S("relbd_in"), 16)
        sp.dma_start(gqk[:, DH:2 * DH], I["k_gain"][0:1, :].broadcast_to([P, DH])).then_inc(S("relbd_in"), 16)

        load_x(fixed(1))
        for part in range(3):
            sp.dma_start(wA[:, :, AD * part:AD * part + AD],
                         w_in_r[:, :, AD * part:AD * part + AD]).then_inc(S(f"wA_in{part}"), 16)
        over_tiles(sp, lambda prev, cur, nxt: load_x(nxt) if prev is not None and nxt is not None else None)

        sp.wait_ge(S("brev_out"), 16)
        for q in range(CC):
            if q >= 2:
                sp.wait_ge(S("cB_full"), 3 * (q - 1))
            sp.dma_start(wB[q % 2], w_conv_r[:, :, 3:6, q, :]).then_inc(S(f"wB_in{q % 2}"), 16)

        sp.wait_ge(S("prj_full"), 3 * TILES)

        def load_z(hd, s):
            sp.dma_start(Z[s], bass.AP(brev.tensor, ZLEN * hd, [[1, P], [1, SEQ]])).then_inc(S(f"att_in{s}"), 16)

        for s in range(4):
            load_z(s, s)
        for pair in range(2):
            sp.wait_ge(S("scored"), 16 * (pair + 1))
            for s in (2 * pair, 2 * pair + 1):
                load_z(4 + s, s)

        sp.wait_ge(S("cB_full"), 3 * CC)
        sp.wait_ge(S("ssc"), 5)
        sp.wait_ge(S("new_out"), 32)
        const(mask, I["c_mask"])
        const(sel, I["c_sel"])
        for g in range(2):
            for kind in range(2):
                for bb in range(4):
                    src = (ck if kind == 0 else cv)[4 * g + bb]
                    if kind == 0 and g == 0:
                        sp.wait_ge(S(f"att_in{bb}"), 32)
                    if kind == 0 and g == 1:
                        sp.wait_ge(S("so_full"), bb + 1)
                    if kind == 1:
                        sp.wait_ge(S("kn_full"), 16 * g + 4 * bb + 4)
                        sp.wait_ge(S("kf_full"), 16 * g + 4 * bb + 4)
                    if kind == 0 and g == 0 and bb == 3:
                        sp.wait_ge(S("scored"), 64)
                    sp.dma_start(KV[bb][:, 0, :, :].rearrange("p a d -> p (a d)"),
                                 src[PAST - NEAR:PAST, :].rearrange("(p a) d -> p (a d)", a=4)).then_inc(S(f"att_in{bb}"), 16)
                    sp.dma_start(KV[bb][0:FAR, 1, :, :].rearrange("p a d -> p (a d)"),
                                 src[0:16 * FAR, :].rearrange("(p a) d -> p (a d)", a=16)[:, 0:NT * AD]).then_inc(S(f"att_in{bb}"), 16)

        sp.wait_ge(S("qst"), 12)
        for c in range(2 * CC):
            sp.dma_start(w_out[:, c, :], I["w_out"][0].rearrange("(c p) n -> p c n", p=P)[:, c, :]).then_inc(S("wout_in"), 16)
        sp.wait_ge(S("sample_done"), 2)
        sp.wait_ge(S("v_out"), 16 * TILES)
        sp.dma_start(gffn, I["g_ffn"][0:1, :].broadcast_to([P, D])).then_inc(S("wout_in"), 16)
        sp.dma_start(w_rt[:, :, 0:GROUPS], I["w_router_group"][0].rearrange("(p c) n -> p c n", c=DC)).then_inc(S("wout_in"), 16)
        sp.dma_start(w_rt[:, :, GROUPS:RG], I["w_router_expert"][0].rearrange("(p c) n -> p c n", c=DC)).then_inc(S("wout_in"), 16)
        sp.dma_start(gple, I["g_ple"][0:1, :].broadcast_to([P, D])).then_inc(S("gple_in"), 16)

        def load_x2(a):
            if not a.early:
                sp.wait_ge(S("h_done"), 2 * a.t - 2)
            sp.dma_start(x_re[a.u][0:a.rows, :], rows_of(xp, xs, a)).then_inc(S(f"in{a.u}"), 16)

        def load_expert(e, s):
            sp.dma_start(SLOTS[s][:, 0:2048], wg_r[e]).then_inc(S(f"w_in{s}"), 16)
            sp.dma_start(SLOTS[s][:, 2048:4096], wu_r[e]).then_inc(S(f"w_in{s}"), 16)
            sp.dma_start(SLOTS[s][:, 4096:6144], wd_r[e]).then_inc(S(f"w_in{s}"), 16)

        load_x2(fixed(0))
        load_expert(0, 0)
        over_tiles(sp, lambda prev, cur, nxt: load_x2(nxt) if nxt is not None else None)

        sp.wait_ge(S("logits_done"), TILES)
        sp.wait_ge(S("out0"), 32 * USES[0])
        sp.wait_ge(S("out1"), 32 * USES[1])
        for s in range(1, 4):
            load_expert(s, s)
        with sp.Fori(0, NE // 4 - 1) as i:
            for s in range(4):
                sp.wait_ge(S("y_full"), 8 * i + 2 * s + 2)
                load_expert(4 * i + 4 + s, s)
        sp.wait_ge(S("routed"), 1)
        for c in range(DC):
            sp.dma_start(w_pg[c], I["w_ple_gate"][0].rearrange("(p c) n -> p c n", c=DC)[:, c, :]).then_inc(S("wpg_in"), 16)

        sp.wait_ge(S("y_full"), 2 * NE)
        over = sp.value_load(small_i[0:1, 0:1], min_val=0, max_val=NOV)
        with sp.If(over > 0):
            for s in range(4):
                load_expert(sp.value_load(ov_e[0:1, s:s + 1], min_val=0, max_val=NE - 1), s)
            with sp.Fori(1, NOV // 4) as i:
                for s in range(4):
                    sp.wait_ge(S("y_full"), 2 * NE + 8 * i + 2 * s - 6)
                    load_expert(sp.value_load(ov_e[0:1, bass.ds(4 * i + s, 1)], min_val=0, max_val=NE - 1), s)
            for u in range(2):
                sp.wait_ge(S(f"rows_out{u}"), 16 * NBLK // 2)
        sp.end_ifs()

        for c in range(2):
            sp.dma_start(w_pp[:, c, :], I["w_ple_proj"][0].rearrange("(p c) n -> p c n", c=2)[:, c, :]).then_inc(S("wpp_in"), 16)

        def load_p(a):
            sp.dma_start(p_in[a.u][0:a.rows, :],
                         rows_of(I["p_prompt"][0, 0], I["p_sample"][0].rearrange("b t d -> (b t) d"), a)).then_inc(S(f"p_in{a.u}"), 16)

        load_p(fixed(0))
        for u in range(2):
            sp.wait_ge(S(f"rows_out{u}"), 16 * NE // 2)

        def load_h(a):
            if not a.early:
                sp.wait_ge(S("h2_done"), a.t - 1)
                sp.wait_ge(S("pT_full"), a.t - 1)
            lo = y_dram[SEQ:TOK, :] if a.rows == SAMP else y_dram[bass.ds(a.t * P, P), :]
            hi = y_dram[TOK + SEQ:2 * TOK, :] if a.rows == SAMP else y_dram[TOK:2 * TOK, :][bass.ds(a.t * P, P), :]
            sp.dma_start(y0[a.u][0:a.rows, :], lo).then_inc(S(f"in{a.u}"), 16)
            sp.dma_start(y1[a.u][0:a.rows, :], hi).then_inc(S(f"in{a.u}"), 16)
            if not a.first:
                load_p(a)

        load_h(fixed(0))
        over_tiles(sp, lambda prev, cur, nxt: load_h(nxt) if nxt is not None else None)

    @block.gpsimd
    def _(pool):
        pool.memset(relbd, 0.0).then_inc(S("relbd_zero"), 1)
        pool.memset(eps, EPS).then_inc(S("ones_set"), 1)
        pool.memset(V[:, :, :, DH:DH + 1], 1.0).then_inc(S("ones_set"), 1)
        pool.memset(ones[:, :], 1.0).then_inc(S("ones_set"), 1)
        pool.memset(lists[0:CAP, :], 4 * TOK).then_inc(S("lists_set"), 1)
        pool.wait_ge(S("lists_set"), 1)
        pool.dma_start(list_dram.rearrange("(s b) c -> s (b c)", b=NBLK), lists[0:CAP, :]).then_inc(S("list_blank"), 16)
        pool.wait_ge(S("bias_done"), 3)
        pool.dma_start(brev, bp).then_inc(S("brev_out"), 16)

        def xt_copy(a):
            pool.wait_ge(S("xT_done"), 2 * a.t + 2)
            pool.tensor_copy(xT[:, :, bass.ds(a.t * P, a.rows)], xTs[a.u][:, :, 0:a.rows]).then_inc(S("xT_kept"), 1)

        def store_kv(a):
            kd = rows_of(O[2], O[5], a)
            vd = rows_of(O[3], O[6], a)
            pool.wait_ge(S("qk_norm"), a.t + 1)
            pool.dma_start(kd, qk[a.u][0:a.rows, AD:2 * AD]).then_inc(S(f"out{a.u}"), 16)
            pool.wait_ge(S("prj_free"), 3 * a.t + 3)
            pool.dma_start(vd.rearrange("r (h d) -> r h d", h=H), V[0:a.rows, a.t, :, 0:DH]).then_inc(S("v_out"), 16)

        def step(prev, cur, nxt):
            if nxt is not None:
                xt_copy(nxt)
            store_kv(cur)

        xt_copy(fixed(0))
        over_tiles(pool, step)

        pool.wait_ge(S("prj_full"), 3 * TILES)
        pool.wait_ge(S("qkT_full"), 2 * TILES)
        pool.wait_ge(S("out0"), 16 * USES[0])
        pool.wait_ge(S("out1"), 16 * USES[1])
        pool.wait_ge(S("xT_kept"), TILES)
        pool.memset(u_p[:, 0:2], 0.0).then_inc(S("pad_zero"), 1)
        pool.wait_ge(S("new_done"), 1)
        pool.dma_start(O[4], new_out[0:2, :]).then_inc(S("new_out"), 16)
        pool.dma_start(O[7], new_out[2:18, :]).then_inc(S("new_out"), 16)

        def copies(a):
            if not a.early:
                pool.wait_ge(S("oC_full"), 2 * a.t - 2)
                pool.wait_ge(S("ss"), a.t + T - 1)
            pool.tensor_copy(at_st[a.u][0:a.rows, :], att[0:a.rows, a.t, :]).then_inc(S("at_copied"), 1)
            pool.tensor_tensor(y_st[a.u][:, :, 0:a.rows], yT[:, :, bass.ds(a.t * P, a.rows)],
                               gconv[:, :].unsqueeze(2).broadcast_to([P, CC, a.rows]), ALU.mult).then_inc(S("y_copied"), 1)

        def store_m(a):
            pool.wait_ge(S("m_done"), a.t + 1)
            pool.dma_start(m_dram[SEQ:TOK, :] if a.rows == SAMP else m_dram[bass.ds(a.t * P, P), :],
                           m_st[a.u][0:a.rows, :]).then_inc(S(f"out{a.u}"), 16)

        pool.wait_ge(S("sample_done"), 2)

        def step_e(prev, cur, nxt):
            if nxt is not None:
                copies(nxt)
            store_m(cur)

        copies(fixed(0))
        over_tiles(pool, step_e)

        pool.wait_ge(S("code_in"), 32)
        pool.wait_ge(S("list_blank"), 16)
        pool.memset(xg[0], 0.0).then_inc(S("xg_zero"), 1)
        pool.memset(xg[1], 0.0).then_inc(S("xg_zero"), 1)
        for k in range(2):
            pool.wait_ge(S("pos_done"), k + 1)
            for t in range(TILES):
                n = P if t < PT else SAMP
                pool.indirect_dma_start(out=list_dram, out_offset=bass.IndirectOffsetOnAxis(ap=pos_i[0:n, TILES * k + t:TILES * k + t + 1], axis=0),
                                        in_=code[0:n, 4 * t + 2 * k:4 * t + 2 * k + 2], in_offset=None,
                                        bounds_check=CAP * NBLK - 1, oob_is_err=False).then_inc(S("list_out"), 16)
        pool.wait_ge(S("list_out"), 16 * 2 * TILES)
        pool.dma_start(lists[0:CAP, :], list_dram.rearrange("(s b) c -> s (b c)", b=NBLK)).then_inc(S("lists_in"), 16)
        pool.wait_ge(S("lists_in"), 16)
        pool.wait_ge(S("out0"), 32 * USES[0])
        pool.wait_ge(S("out1"), 32 * USES[1])
        pool.wait_ge(S("xg_zero"), 2)

        def gather(n, u):
            if not (isinstance(n, int) and n < 2):
                pool.wait_ge(S("rowsT_full"), 2 * n - 2)
            pool.tensor_copy(idx_c[0:CAP, u:u + 1], lists[0:CAP, bass.ds(2 * n, 1)]).then_inc(S("src_idx"), 1)
            pool.wait_ge(S("src_idx"), n + 1)
            waits_end(pool, S("pool_seen"))
            pool.indirect_dma_start(out=xg[u], out_offset=None, in_=m_dram,
                                    in_offset=bass.IndirectOffsetOnAxis(ap=idx_c[0:CAP, u:u + 1], axis=0),
                                    bounds_check=TOK - 1, oob_is_err=False).then_inc(S(f"rows_in{u}"), 16)

        def scatter(n, u, k):
            if not (isinstance(n, int) and n < 2):
                pool.wait_ge(S(f"rows_out{u}"), 16 * k)
            pool.tensor_copy(idx_c[0:CAP, 2 + u:3 + u], lists[0:CAP, bass.ds(2 * n + 1, 1)]).then_inc(S("dst_idx"), 1)
            pool.wait_ge(S("dst_idx"), n + 1)
            pool.wait_ge(S("rows_done"), 2 * n + 2)
            waits_end(pool, S("pool_seen"))
            pool.indirect_dma_start(out=y_dram, out_offset=bass.IndirectOffsetOnAxis(ap=idx_c[0:CAP, 2 + u:3 + u], axis=0),
                                    in_=yo[u], in_offset=None,
                                    bounds_check=2 * TOK - 1, oob_is_err=False).then_inc(S(f"rows_out{u}"), 16)

        def exchange(first, count):
            for n in range(4):
                gather(first + n, n % 2)
            for u in range(2):
                gather(first + 4 + u, u)
                scatter(first + u, u, first // 2)
            with pool.Fori(first // 2 + 1, (first + count) // 2 - 2) as i:
                for u in range(2):
                    gather(2 * i + 4 + u, u)
                    scatter(2 * i + u, u, i)
            for n in range(4):
                scatter(first + count - 4 + n, n % 2, (first + count - 4 + n) // 2)
            for u in range(2):
                pool.wait_ge(S(f"rows_out{u}"), 16 * (first + count) // 2)

        exchange(0, NE)
        over = pool.value_load(small_i[0:1, 0:1], min_val=0, max_val=NOV)
        with pool.If(over > 0):
            exchange(NE, NOV)
        pool.end_ifs()

        def store(a):
            pool.wait_ge(S("out_done"), a.t + 1)
            pool.dma_start(rows_of(O[0], O[1], a), ot[a.u][0:a.rows, :]).then_inc(S(f"out{a.u}"), 16)

        over_tiles(pool, lambda prev, cur, nxt: store(cur))
        pool.wait_ge(S("out0"), 48 * USES[0])
        pool.wait_ge(S("out1"), 48 * USES[1])
        pool.wait_ge(S("v_out"), 16 * TILES)
        pool.wait_ge(S("new_out"), 32)

    @block.scalar
    def _(act):
        def root(out, ss, n):
            return act.activation(out, ss, ACT.Sqrt, bias=eps[0:ss.shape[0], :], scale=1.0 / n)

        act.wait_ge(S("ones_set"), 3)
        def square_x(a):
            act.wait_ge(S(f"in{a.u}"), 16 * (a.k + 1))
            if not a.first:
                act.wait_ge(S("rs_done"), a.t)
            act.activation(junk[0:a.rows, :], x_in[a.u][0:a.rows, :], ACT.Square,
                           accum_out=ssx[0:a.rows, a.u:a.u + 1]).then_inc(S("ss"), 1)
            act.wait_ge(S("ss"), a.t + 1)
            root(ms_x[0:a.rows, a.u:a.u + 1], ssx[0:a.rows, a.u:a.u + 1], D).then_inc(S("ms"), 1)

        def scale_x(a):
            act.wait_ge(S("rs_done"), a.t + 1)
            act.activation(x_in[a.u][0:a.rows, :], x_in[a.u][0:a.rows, :], ACT.Copy,
                           scale=rs_x[0:a.rows, a.u:a.u + 1]).then_inc(S("xn"), 1)

        def evac_qkv(a):
            n = a.rows
            act.wait_ge(S("prj_full"), 3 * a.t + 1)
            if not a.early:
                act.wait_ge(S("qkT_full"), 2 * a.t - 2)
                act.wait_ge(S(f"out{a.u}"), 16 * a.k)
            act.activation(qk[a.u][0:n, 0:AD], bk[4][0:n, :], ACT.Copy).then_inc(S("prj_free"), 1)
            act.wait_ge(S("prj_full"), 3 * a.t + 2)
            act.activation(qk[a.u][0:n, AD:2 * AD], bk[5][0:n, :], ACT.Copy).then_inc(S("prj_free"), 1)
            act.wait_ge(S("prj_full"), 3 * a.t + 3)
            act.activation(V[0:n, a.t, :, 0:DH], bk[6][0:n, :].rearrange("p (h d) -> p h d", h=H), ACT.Copy).then_inc(S("prj_free"), 1)
            act.wait_ge(S("prj_free"), 3 * a.t + 2)
            if not a.first:
                act.wait_ge(S("hd_sum"), a.t)
            act.activation(qk_sq[0:n, :], qk[a.u][0:n, :], ACT.Square).then_inc(S("qk_sq"), 1)
            act.wait_ge(S("hd_sum"), a.t + 1)
            root(hd_r[0:n, :], hd_s[0:n, :], DH).then_inc(S("mean"), 1)

        def evac_qkT(a):
            n = a.rows
            act.wait_ge(S("qkT_full"), 2 * a.t + 1)
            dq = qts[:, :, :] if n == SAMP else QT[:, :, bass.ds(a.t * P, P)]
            dk = kts[:, :, :] if n == SAMP else KT[:, :, bass.ds(a.t * P, P)]
            src = bk[2].rearrange("p (g n) -> p g n", g=NG)
            if n == P:
                src = src[:, :, ::-1]
            act.activation(dq, src[:, :, 0:n], ACT.Copy).then_inc(S("qkT_free"), 1)
            act.wait_ge(S("qkT_full"), 2 * a.t + 2)
            act.activation(dk, bk[3].rearrange("p (g n) -> p g n", g=NG)[:, :, 0:n], ACT.Copy).then_inc(S("qkT_done"), 1)

        square_x(fixed(0))
        scale_x(fixed(0))

        def step(prev, cur, nxt):
            if nxt is not None:
                square_x(nxt)
                scale_x(nxt)
            evac_qkv(cur)
            if prev is not None:
                evac_qkT(prev)

        over_tiles(act, step)
        evac_qkT(fixed(8))

        for q in range(CC):
            for j, (lo, n) in enumerate(((0, 512), (512, 512), (SEQ, SAMP))):
                act.wait_ge(S("cC_full"), 3 * q + j + 1)
                if q >= 1 and j == 0:
                    act.wait_ge(S("u_done"), 3 * q)
                if q == 0 and j == 0:
                    act.wait_ge(S("xT_kept"), TILES)
                    act.wait_ge(S("prj_full"), 3 * TILES)
                act.activation(c_sb[:, lo:lo + n], bk[(3 * q + j) % 2][:, 0:n], ACT.Copy).then_inc(S("cC_done"), 1)
            act.wait_ge(S("y_done"), 3 * (q + 1))
            if q >= 1:
                act.wait_ge(S("y_sum"), q)
            act.activation(y_sq, yT[:, q, :], ACT.Square).then_inc(S("y_sq"), 1)
        act.wait_ge(S("ssc"), 3)
        root(rc, ssc, CD).then_inc(S("ssc"), 1)

        with act.Fori(0, 2) as it:
            for pp in range(2):
                def exp(n):
                    hh, i = ORDER[n]
                    act.wait_ge(S("scored"), 32 * it + 16 * pp + n + 1)
                    w = P * (i + 1)
                    act.activation(Eb[n % 2][:, 0:w], Eb[n % 2][:, 0:w], ACT.Exp, bias=nmax[:, n % 2:n % 2 + 1],
                                   scale=-1.0).then_inc(S("exp_done"), 1)

                t_use = [0]

                def evac_pt(n):
                    hh, i = ORDER[n]
                    act.wait_ge(S("ot_full"), 32 * it + 16 * pp + (n - 1 if n >= 2 else 0))
                    for j0 in range(0, i + 1, 4):
                        m = min(4, i + 1 - j0)
                        act.wait_ge(S("tp_full"), 48 * it + 24 * pp + t_use[0] + 1)
                        act.activation(PTb[n % 2][:, j0:j0 + m, :],
                                       bk[4 + t_use[0] % 2].rearrange("p (a b) -> p a b", b=P)[:, 0:m, ::-1],
                                       ACT.Copy).then_inc(S("tp_free"), 1)
                        t_use[0] += 1

                exp(0)
                exp(1)
                for n in range(16):
                    evac_pt(n)
                    if n + 2 < 16:
                        exp(n + 2)

        with act.Fori(0, 2) as g:
            for bb in range(4):
                for gg in range(NG):
                    act.wait_ge(S("kn_full"), 16 * g + 4 * bb + gg + 1)
                    if gg == 0:
                        act.wait_ge(S("ss_done"), 4 * g + bb)
                    act.activation(ktc[:, gg, 0:NEAR], bk[2 + gg % 2], ACT.Copy).then_inc(S("kn_free"), 1)
            act.wait_ge(S("ss_scored"), g + 1)
            act.activation(Es, Es, ACT.Exp, bias=nms, scale=-1.0, accum_out=dens).then_inc(S("ss_exp"), 1)
            act.wait_ge(S("st_full"), 3 * g + 1)
            act.activation(PTs[:, 0:4, :].rearrange("p a b -> p (a b)"), bk[2], ACT.Copy).then_inc(S("st_done"), 1)
            act.wait_ge(S("st_full"), 3 * g + 2)
            act.activation(PTs[0:FAR, 4:8, :].rearrange("p a b -> p (a b)"), bk[3][0:FAR, :], ACT.Copy).then_inc(S("st_done"), 1)
            act.wait_ge(S("st_full"), 3 * g + 3)
            act.activation(PTs[0:SAMP, 8, :], bk[4][0:SAMP, 0:P], ACT.Copy).then_inc(S("st_done"), 1)

        def square_att(a):
            act.wait_ge(S("at_copied"), a.t + 1)
            if not a.first:
                act.wait_ge(S("ra_done"), a.t)
            act.activation(junkE[0:a.rows, 0:AD], at_st[a.u][0:a.rows, :], ACT.Square,
                           accum_out=ssa[0:a.rows, a.u:a.u + 1]).then_inc(S("ss"), 1)
            act.wait_ge(S("ss"), a.t + T + 1)
            root(msa[0:a.rows, a.u:a.u + 1], ssa[0:a.rows, a.u:a.u + 1], AD).then_inc(S("ms"), 1)

        def square_h(a):
            act.wait_ge(S("h_done"), 2 * a.t + 2)
            act.activation(junkE[0:a.rows, :], h[0:a.rows, a.t, :], ACT.Square,
                           accum_out=ssh[0:a.rows, a.u:a.u + 1]).then_inc(S("ssh"), 1)
            act.wait_ge(S("ssh"), a.t + 1)
            root(msh[0:a.rows, a.u:a.u + 1], ssh[0:a.rows, a.u:a.u + 1], D).then_inc(S("mean"), 1)

        def evac_mT(a):
            n = a.rows
            for j in range(2):
                act.wait_ge(S("xT_full"), 2 * (a.t + T) + j + 1)
                act.activation(mT[a.u][:, 4 * j:4 * j + 4, 0:n],
                               bk[5 + j].rearrange("p (g n) -> p g n", g=4)[:, :, 0:n], ACT.Copy).then_inc(S("mT_done"), 1)

        def step_e(prev, cur, nxt):
            if nxt is not None:
                square_att(nxt)
            if prev is not None:
                evac_mT(prev)
            square_h(cur)

        square_att(fixed(0))
        over_tiles(act, step_e)
        evac_mT(fixed(8))

        act.wait_ge(S("r_shift"), 2)
        act.activation(r_ge, r_ge, ACT.Exp).then_inc(S("r_exp"), 1)
        act.activation(r_e2, r_e2, ACT.Exp).then_inc(S("r_exp"), 1)

        def block_act(n, u, k):
            act.wait_ge(S("gu_full"), n + 1)
            gbank = bk[2 + u][:, 0:4 * CAP].rearrange("p (s j n) -> p s j n", s=2, j=2)
            act.activation(sg[u], gbank[:, 0], ACT.Silu).then_inc(S("silu"), 1)
            act.wait_ge(S("y_full"), 2 * n + 1)
            if not (isinstance(n, int) and n < 2):
                act.wait_ge(S(f"rows_out{u}"), 16 * k)
            act.activation(yo[u][:, 0:512], bk[4 + 2 * u][0:CAP, :], ACT.Copy).then_inc(S("rows_done"), 1)
            act.wait_ge(S("y_full"), 2 * n + 2)
            act.activation(yo[u][:, 512:1024], bk[5 + 2 * u][0:CAP, :], ACT.Copy).then_inc(S("rows_done"), 1)

        block_act(0, 0, 0)
        block_act(1, 1, 0)
        with act.Fori(1, NE // 2) as i:
            for u in range(2):
                block_act(2 * i + u, u, i)
        over = act.value_load(small_i[0:1, 0:1], min_val=0, max_val=NOV)
        with act.If(over > 0):
            with act.Fori(NE // 2, NBLK // 2) as i:
                for u in range(2):
                    block_act(2 * i + u, u, i)
        act.end_ifs()

        def square_f(a):
            act.wait_ge(S("h2_done"), a.t + 1)
            act.activation(junkH[0:a.rows, :], h2[a.u][0:a.rows, :], ACT.Square,
                           accum_out=ssf[0:a.rows, a.u:a.u + 1]).then_inc(S("ss"), 1)
            act.wait_ge(S("ss"), a.t + 2 * T + 1)
            root(msf[0:a.rows, a.u:a.u + 1], ssf[0:a.rows, a.u:a.u + 1], D).then_inc(S("ms"), 1)

        def evac_pT(a):
            n = a.rows
            act.wait_ge(S("pT_full"), a.t + 1)
            act.activation(pT[a.u][:, :, 0:n], bk[6][:, 0:2 * P].rearrange("p (g n) -> p g n", g=2)[:, :, 0:n],
                           ACT.Copy).then_inc(S("pT_done"), 1)

        def evac_hnT(a):
            n = a.rows
            for j in range(2):
                act.wait_ge(S("xT_full"), 2 * (a.t + 2 * T) + j + 1)
                act.activation(hnT[a.u][:, 4 * j:4 * j + 4, 0:n],
                               bk[j].rearrange("p (g n) -> p g n", g=4)[:, :, 0:n], ACT.Copy).then_inc(S("mT_done"), 1)

        def gate(a):
            n = a.rows
            for j in range(2):
                act.wait_ge(S("gate_full"), 2 * a.t + j + 1)
                if j == 0 and not a.early:
                    act.wait_ge(S("out_done"), a.t - 1)
                act.activation(gs[a.u][0:n, 512 * j:512 * j + 512], bk[2 + j][0:n, :], ACT.Sigmoid).then_inc(S("gate_done"), 1)

        def step_h(prev, cur, nxt):
            if nxt is not None:
                square_f(nxt)
            gate(cur)
            if nxt is not None:
                evac_pT(nxt)
                evac_hnT(nxt)

        evac_pT(fixed(0))
        square_f(fixed(0))
        evac_hnT(fixed(0))
        over_tiles(act, step_h)

    @block.vector
    def _(dve):
        dve.wait_ge(S("const_in"), 16 * NCONST)
        for j in range(3):
            dve.wait_ge(S("bias_full"), j + 1)
            c = slice(384 * j, 384 * j + 384)
            dve.tensor_tensor(bp[:, c], bk[4 + j][0:H, 0:384], logp[:, c], ALU.add).then_inc(S("bias_done"), 1)
        dve.wait_ge(S("bias_full"), 4)
        dve.tensor_tensor(bias_s[:, 0:512], bk[2], bias_s[:, 0:512], ALU.add).then_inc(S("bias_done"), 1)
        dve.wait_ge(S("bias_full"), 5)
        dve.tensor_tensor(bias_s[:, 512:SK], bk[3][:, 0:SK - 512], bias_s[:, 512:SK], ALU.add).then_inc(S("bias_done"), 1)
        dve.tensor_tensor(bias_new[:, :], bk[3][:, SK - 512:SK - 512 + 2 * SAMP], bias_new[:, :], ALU.add).then_inc(S("bias_done"), 1)
        dve.wait_ge(S("bias_full"), 6)
        dve.tensor_copy(stT[:, :], bk[7][:, 0:64]).then_inc(S("bias_done"), 1)
        dve.wait_ge(S("relbd_in"), 16 * 5)
        dve.tensor_scalar(gqk[:, 0:DH], gqk[:, 0:DH], DH ** -0.5, None, ALU.mult).then_inc(S("gq_done"), 1)

        def rstd(a):
            n, u = a.rows, a.u
            dve.wait_ge(S("ms"), a.t + 1)
            dve.reciprocal(rs_x[0:n, u:u + 1], ms_x[0:n, u:u + 1]).then_inc(S("rs_done"), 1)

        def evac_xT(a):
            n = a.rows
            if not a.early:
                dve.wait_ge(S("prj_full"), 3 * a.t - 3)
                dve.wait_ge(S("xT_kept"), a.t - 1)
            for j in range(2):
                dve.wait_ge(S("xT_full"), 2 * a.t + j + 1)
                ins = dve.tensor_tensor(xTs[a.u][:, 4 * j:4 * j + 4, 0:n],
                                        bk[j].rearrange("p (g n) -> p g n", g=4)[:, :, 0:n],
                                        gmix[:, 4 * j:4 * j + 4].unsqueeze(2).broadcast_to([P, 4, n]), ALU.mult)
                ins.then_inc(S("xT_done"), 1)

        def qk_norm(a):
            n, u = a.rows, a.u
            dve.wait_ge(S("qk_sq"), a.t + 1)
            dve.tensor_reduce(hd_s[0:n, :], qk_sq[0:n, :].rearrange("p (h d) -> p h d", d=DH), AX.X, ALU.add).then_inc(S("hd_sum"), 1)
            dve.wait_ge(S("mean"), a.t + 1)
            dve.reciprocal(hd_q[0:n, :], hd_r[0:n, :]).then_inc(S("rstd"), 1)
            dve.wait_ge(S("rstd"), a.t + 1)
            v = qk[u][0:n, :].rearrange("p (h d) -> p h d", d=DH)
            dve.tensor_tensor(v, v, hd_q[0:n, :].unsqueeze(2).broadcast_to([n, 2 * H, DH]), ALU.mult).then_inc(S("scaled"), 1)
            dve.wait_ge(S("scaled"), a.t + 1)
            w = qk[u][0:n, :].rearrange("p (s h d) -> p s h d", s=2, d=DH)
            dve.tensor_tensor(w, w, gqk[0:n, :].rearrange("p (s d) -> p s d", s=2).unsqueeze(2).broadcast_to([n, 2, H, DH]),
                              ALU.mult).then_inc(S("qk_norm"), 1)

        def step(prev, cur, nxt):
            if nxt is not None:
                rstd(nxt)
                evac_xT(nxt)
            qk_norm(cur)

        dve.wait_ge(S("gq_done"), 1)
        rstd(fixed(0))
        evac_xT(fixed(0))
        over_tiles(dve, step)

        wj = convw[:, :].rearrange("p (j c) -> p j c", j=3)
        ysv = yT[:, :, SEQ:TOK]
        dve.wait_ge(S("pad_zero"), 1)
        for q in range(CC):
            if q == 0:
                dve.wait_ge(S("qkT_full"), 2 * TILES)
                dve.wait_ge(S("out0"), 16 * USES[0])
                dve.wait_ge(S("out1"), 16 * USES[1])
                dve.wait_ge(S("xT_kept"), TILES)
            dve.tensor_copy(u_s[:, :, 0:2], stT[:, 16 * q:16 * q + 16].rearrange("p (b j) -> p b j", j=2)).then_inc(S("us_pad"), 1)
            for j, (lo, n) in enumerate(((0, 512), (512, 512), (SEQ, SAMP))):
                dve.wait_ge(S("ch_full"), 3 * q + j + 1)
                dve.wait_ge(S("cC_done"), 3 * q + j + 1)
                src = bk[2 + (3 * q + j) % 2]
                if j < 2:
                    dve.tensor_tensor(u_p[:, 2 + lo:2 + lo + n], src, c_sb[:, lo:lo + n], ALU.mult).then_inc(S("u_done"), 1)
                else:
                    dve.tensor_tensor(u_s[:, :, 2:NT + 2], src[:, 0:SAMP].rearrange("p (b t) -> p b t", t=NT),
                                      c_sb[:, SEQ:TOK].rearrange("p (b t) -> p b t", t=NT), ALU.mult).then_inc(S("u_done"), 1)
            dve.wait_ge(S("u_done"), 3 * q + 3)
            dve.wait_ge(S("us_pad"), q + 1)
            dve.tensor_copy(u_new[:, 18 * q:18 * q + 2], u_p[:, SEQ:SEQ + 2]).then_inc(S("unew"), 1)
            dve.tensor_copy(u_new[:, 18 * q + 2:18 * q + 18].rearrange("p (b j) -> p b j", j=2),
                            u_s[:, :, NT:NT + 2]).then_inc(S("unew"), 1)
            cs = conv[:, SEQ:TOK].rearrange("p (b t) -> p b t", t=NT)
            for j in range(3):
                w = wj[:, j, q:q + 1]
                if j == 0:
                    dve.tensor_scalar(conv[:, 0:SEQ], u_p[:, 0:SEQ], w, None, ALU.mult).then_inc(S("conv"), 1)
                    dve.tensor_scalar(cs, u_s[:, :, 0:NT], w, None, ALU.mult).then_inc(S("conv"), 1)
                else:
                    dve.wait_ge(S("conv"), 6 * q + 2 * j)
                    dve.scalar_tensor_tensor(conv[:, 0:SEQ], u_p[:, j:j + SEQ], w, conv[:, 0:SEQ], ALU.mult, ALU.add).then_inc(S("conv"), 1)
                    dve.scalar_tensor_tensor(cs, u_s[:, :, j:j + NT], w, cs, ALU.mult, ALU.add).then_inc(S("conv"), 1)
            dve.wait_ge(S("conv"), 6 * q + 6)
            if q == 0:
                dve.wait_ge(S("hd_sum"), TILES)
            for j, (lo, n) in enumerate(((0, 512), (512, 512), (SEQ, SAMP))):
                dve.wait_ge(S("cB_full"), 3 * q + j + 1)
                dve.tensor_tensor(yT[:, q, lo:lo + n], bk[4 + j][:, 0:n], conv[:, lo:lo + n], ALU.mult).then_inc(S("y_done"), 1)
            dve.wait_ge(S("y_sq"), q + 1)
            if q == 0:
                dve.tensor_copy(y_sum, y_sq).then_inc(S("y_sum"), 1)
            else:
                dve.wait_ge(S("y_sum"), q)
                dve.tensor_tensor(y_sum, y_sum, y_sq, ALU.add).then_inc(S("y_sum"), 1)
        dve.wait_ge(S("new_full"), 1)
        dve.tensor_copy(new_out, bk[0][0:18, :]).then_inc(S("new_done"), 1)
        dve.wait_ge(S("ssc_full"), 1)
        dve.memset(ssc, 1.0).then_inc(S("ssc"), 1)
        dve.wait_ge(S("ssc"), 1)
        dve.tensor_copy(ssc[:, 0:PT], bk[7][:, 0:PT]).then_inc(S("ssc"), 1)
        dve.tensor_copy(ssc[0:SAMP, PT:TILES], bk[7][0:SAMP, PT:TILES]).then_inc(S("ssc"), 1)
        dve.wait_ge(S("ssc"), 4)
        dve.reciprocal(rc, rc).then_inc(S("ssc"), 1)

        dve.wait_ge(S("qkT_done"), TILES)
        def take_pair(pair, pp):
            dve.tensor_copy(qst[pp], QT[:, pair, :]).then_inc(S("qst"), 1)
            dve.tensor_copy(kst[pp], KT[:, pair, :]).then_inc(S("qst"), 1)
            dve.tensor_copy(vst[pp], V[:, 0:PT, bass.ds(2 * pair, 2), :]).then_inc(S("qst"), 1)

        with dve.Fori(0, 2) as it:
            for pp in range(2):
                base = 32 * it + 16 * pp
                if pp == 0:
                    take_pair(2 * it, 0)

                def bias(n):
                    hh, i = ORDER[n]
                    w = P * (i + 1)
                    if n < 2:
                        dve.wait_ge(S(f"att_in{2 * pp + hh}"), 16 * (it + 1))
                    dve.wait_ge(S("s_full"), base + n + 1)
                    dve.wait_ge(S("tp_full"), 24 * (2 * it + pp) + (tp_uses(n - 1) if n >= 2 else 0))
                    waits_end(dve, S("dve_seen"))
                    dve.tensor_tensor_reduce(Eb[n % 2][:, 0:w], bank[n % 2][:, 0:w], Z[2 * pp + hh][:, SEQ - w:SEQ], -1.0, 3e38,
                                             ALU.add, ALU.min, nmax[:, n % 2:n % 2 + 1]).then_inc(S("scored"), 1)

                def copy_ot(n):
                    dve.wait_ge(S("ot_full"), base + n + 1)
                    dve.tensor_copy(OT[n % 2], bk[6][0:DH + 1, 0:P]).then_inc(S("ot_copied"), 1)

                def evac_o(n):
                    hh, i = ORDER[n]
                    dve.wait_ge(S("o_full"), base + n + 1)
                    dve.reciprocal(rden[:, n:n + 1], bk[7][:, DH:DH + 1]).then_inc(S("rden"), 1)
                    dve.wait_ge(S("rden"), base + n + 1)
                    dve.tensor_scalar(att[:, i, bass.ds((4 * it + 2 * pp + hh) * DH, DH)], bk[7][:, 0:DH],
                                      rden[:, n:n + 1], None, ALU.mult).then_inc(S("o_free"), 1)

                bias(0)
                bias(1)
                for n in range(16):
                    if n + 2 < 16:
                        bias(n + 2)
                    if n >= 1:
                        copy_ot(n - 1)
                    if n >= 2:
                        evac_o(n - 2)
                    if n == 8 and pp == 0:
                        take_pair(2 * it + 1, 1)
                copy_ot(15)
                evac_o(14)
                evac_o(15)

        dve.wait_ge(S("o_full"), 64)
        dve.memset(qbd, 0.0).then_inc(S("qbd_zero"), 1)
        dve.memset(att[0:SAMP, PT, :], 0.0).then_inc(S("qbd_zero"), 1)
        dve.wait_ge(S("qbd_zero"), 2)
        dve.wait_ge(S("const_in"), 16 * (NCONST + 2))
        with dve.Fori(0, 2) as g:
            dve.wait_ge(S("ss_done"), 4 * g)
            for hd in range(H):
                gg, lo = hd // 2, 64 * (hd % 2)
                dve.tensor_copy(qbd[lo:lo + 64, :, gg, :, hd],
                                qts[lo:lo + 64, gg, bass.ds(16 * g, 16)].rearrange("p (b t) -> p b t", t=NT)).then_inc(S("qbd"), 1)
            dve.tensor_copy(sel_st, sel[:, g, :]).then_inc(S("qbd"), 1)
            dve.tensor_copy(bias_s[:, SK:SKN], bias_new[:, bass.ds(SAMP * g, SAMP)]).then_inc(S("qbd"), 1)
            for bb in range(4):
                for gg in range(NG):
                    dve.wait_ge(S("kf_full"), 16 * g + 4 * bb + gg + 1)
                    if gg == 0:
                        dve.wait_ge(S("ss_done"), 4 * g + bb)
                    dve.tensor_copy(ktc[:, gg, NEAR:SK], bk[4 + gg % 2][:, 0:NT * FAR]).then_inc(S("kf_free"), 1)
            dve.wait_ge(S("ss_done"), 4 * g + 4)
            dve.wait_ge(S("qbd"), 10 * g + 10)
            waits_end(dve, S("dve_seen"))
            dve.tensor_tensor_reduce(Es, bank[0][:, 0:SKN], bias_s[:, :], -1.0, 3e38, ALU.add, ALU.min, nms).then_inc(S("ss_scored"), 1)
            dve.wait_ge(S("ss_exp"), g + 1)
            dve.reciprocal(rdens, dens).then_inc(S("rdens"), 1)
            dve.wait_ge(S("rdens"), g + 1)
            dve.wait_ge(S("so_full"), 4 * g + 4)
            dve.scalar_tensor_tensor(masked, bk[6], rdens, mask, ALU.mult, ALU.mult).then_inc(S("masked"), 1)
            dve.wait_ge(S("sum_full"), g + 1)
            dve.tensor_tensor(att[0:SAMP, PT, :], bk[7][0:SAMP, :], att[0:SAMP, PT, :], ALU.add).then_inc(S("sample_done"), 1)
            dve.wait_ge(S("sample_done"), g + 1)

        def ra_of(a):
            n, u = a.rows, a.u
            dve.wait_ge(S("ms"), a.t + T + 1)
            dve.reciprocal(ra[0:n, u:u + 1], msa[0:n, u:u + 1]).then_inc(S("ra_done"), 1)

        def evac_atT(a):
            n = a.rows
            dve.wait_ge(S("atT_full"), a.t + 1)
            dve.tensor_tensor(atT[a.u][:, :, 0:n], bk[4].rearrange("p (g n) -> p g n", g=CC)[:, :, 0:n],
                              gatt[:, :].unsqueeze(2).broadcast_to([P, CC, n]), ALU.mult).then_inc(S("atT_done"), 1)

        def residual(a):
            n, u = a.rows, a.u
            dve.wait_ge(S(f"in{u}"), 16 * (a.k + 1 + USES[u]))
            dve.wait_ge(S("ra_done"), a.t + 1)
            for j in range(2):
                c = slice(512 * j, 512 * j + 512)
                dve.wait_ge(S("oA_full"), 2 * a.t + j + 1)
                dve.scalar_tensor_tensor(x_re[u][0:n, c], bk[j][0:n, :], ra[0:n, u:u + 1], x_re[u][0:n, c],
                                         ALU.mult, ALU.add).then_inc(S("hA_done"), 1)
            for j in range(2):
                c = slice(512 * j, 512 * j + 512)
                dve.wait_ge(S("oC_full"), 2 * a.t + j + 1)
                dve.wait_ge(S("hA_done"), 2 * a.t + j + 1)
                dve.scalar_tensor_tensor(h[0:n, a.t, c], bk[2 + j][0:n, :], rc[0:n, bass.ds(a.t, 1)], x_re[u][0:n, c],
                                         ALU.mult, ALU.add).then_inc(S("h_done"), 1)

        def make_m(a):
            n, u = a.rows, a.u
            dve.wait_ge(S("mean"), a.t + T + 1)
            dve.reciprocal(rsh[0:n, u:u + 1], msh[0:n, u:u + 1]).then_inc(S("rstd"), 1)
            dve.wait_ge(S("rstd"), a.t + T + 1)
            if not a.early:
                dve.wait_ge(S("xT_full"), 2 * (a.t + T) - 2)
                dve.wait_ge(S(f"out{u}"), 16 * (a.k + USES[u]))
            dve.scalar_tensor_tensor(m_st[u][0:n, :], h[0:n, a.t, :], rsh[0:n, u:u + 1], gffn[0:n, :],
                                     ALU.mult, ALU.mult).then_inc(S("m_done"), 1)

        def take_logits(a):
            n = a.rows
            dve.wait_ge(S("lg_full"), a.t + 1)
            dve.tensor_copy(lg[0:n, a.t, :], bk[7][0:n, 0:RG]).then_inc(S("logits_done"), 1)

        def step_e(prev, cur, nxt):
            if nxt is not None:
                ra_of(nxt)
                evac_atT(nxt)
            residual(cur)
            make_m(cur)
            if prev is not None:
                take_logits(prev)

        dve.memset(lg, 0.0).then_inc(S("lg_zero"), 1)
        dve.wait_ge(S("wout_in"), 16 * (2 * CC + 3))
        dve.wait_ge(S("lg_zero"), 1)
        ra_of(fixed(0))
        evac_atT(fixed(0))
        over_tiles(dve, step_e)
        take_logits(fixed(8))
        dve.wait_ge(S("logits_done"), TILES)
        dve.wait_ge(S("code_in"), 32)

        seq = [0]

        def then(ins):
            seq[0] += 1
            ins.then_inc(S("r_step"), 1)
            dve.wait_ge(S("r_step"), seq[0])

        G2, EE = GROUPS, NE
        iota = misc[:, 0:NE]

        def bc(ap, n):
            return ap.unsqueeze(2).broadcast_to([P, ap.shape[1], n])

        def first_max(val, width, mx, hot, idx):
            then(dve.tensor_reduce(mx, val, AX.X, ALU.max))
            then(dve.tensor_tensor(hot, val, bc(mx, width), ALU.is_equal))
            it = iota[:, 0:width].unsqueeze(1).broadcast_to([P, T, width])
            then(dve.tensor_scalar(hot, hot, -100.0, 100.0, ALU.mult, ALU.add))
            then(dve.tensor_tensor(hot, hot, it, ALU.add))
            then(dve.tensor_reduce(idx, hot, AX.X, ALU.min))
            then(dve.tensor_tensor(hot, it, bc(idx, width), ALU.is_equal))

        lgG, lgE = lg[:, :, 0:G2], lg[:, :, G2:RG]
        first_max(lgG, G2, r_mg, r_hg, r_ig)
        dve.tensor_tensor(r_ge, lgG, bc(r_mg, G2), ALU.subtract).then_inc(S("r_shift"), 1)
        e4 = lgE.rearrange("p t (g e) -> p t g e", e=EPG)
        m4 = r_ms.rearrange("p t (g e) -> p t g e", e=EPG)
        hg4 = r_hg.unsqueeze(3).broadcast_to([P, T, G2, EPG])
        then(dve.tensor_tensor(m4, e4, hg4, ALU.mult))
        then(dve.tensor_scalar(r_hg2, r_hg, -NEG, NEG, ALU.mult, ALU.add))
        then(dve.tensor_tensor(m4, m4, r_hg2.unsqueeze(3).broadcast_to([P, T, G2, EPG]), ALU.add))
        first_max(r_ms, EE, r_m1, r_h1, r_i1)
        then(dve.tensor_scalar(r_t, r_h1, NEG, None, ALU.mult))
        then(dve.tensor_tensor(r_ms, r_ms, r_t, ALU.add))
        first_max(r_ms, EE, r_m2, r_h2, r_i2)
        dve.tensor_tensor(r_e2, r_m2, r_m1, ALU.subtract).then_inc(S("r_shift"), 1)
        for hot in (r_h1, r_h2):
            then(dve.tensor_scalar(hot[:, PT, :], hot[:, PT, :], misc[:, 63:64], None, ALU.mult))
        then(dve.tensor_tensor(r_t, r_h1, r_h2, ALU.add))
        dve.tensor_copy(r_a, r_t).then_inc(S("r_sum"), 1)
        dve.wait_ge(S("rank_full"), 1)
        then(dve.tensor_copy(r_tot, bk[0][:, 0:T * EE].rearrange("p (t e) -> p t e", e=EE)))
        dve.wait_ge(S("rank_full"), 2)
        then(dve.tensor_copy(r_rank, bk[1][:, 0:T * EE].rearrange("p (t e) -> p t e", e=EE)))
        then(dve.memset(r_cum[:, 0, :], 0.0))
        for t in range(1, T + 1):
            then(dve.tensor_tensor(r_cum[:, t, :], r_cum[:, t - 1, :], r_tot[:, t - 1, :], ALU.add))
        then(dve.tensor_tensor(r_rank, r_rank, r_cum[:, 0:T, :], ALU.add))
        th = misc[:, NE:NE + NTH - 1]
        then(dve.tensor_tensor(r_big, r_cum[:, T, :].unsqueeze(2).broadcast_to([P, EE, NTH - 1]),
                               th.unsqueeze(1).broadcast_to([P, EE, NTH - 1]), ALU.is_gt))
        then(dve.tensor_reduce(r_ov[:, 0, :], r_big, AX.X, ALU.add))
        then(dve.tensor_copy(r_ov[:, 1, :], r_ov[:, 0, :]))
        src, dst = 1, 2
        for s in (1, 2, 4, 8, 16):
            then(dve.tensor_copy(r_ov[:, dst, 0:s], r_ov[:, src, 0:s]))
            then(dve.tensor_tensor(r_ov[:, dst, s:EE], r_ov[:, src, s:EE], r_ov[:, src, 0:EE - s], ALU.add))
            src, dst = dst, src
        incl = r_ov[:, src, :]
        then(dve.tensor_tensor(r_ov[:, 3, :], incl, r_ov[:, 0, :], ALU.subtract))
        then(dve.tensor_tensor(r_bb, incl.unsqueeze(1).broadcast_to([P, NOV, EE]),
                               blk[:, :].unsqueeze(2).broadcast_to([P, NOV, EE]), ALU.is_le))
        then(dve.tensor_reduce(r_be, r_bb, AX.X, ALU.add))
        then(dve.tensor_scalar(ov_e[:, :], r_be, float(NE - 1), None, ALU.min))
        then(dve.tensor_copy(small_i[:, 0:1], incl[:, EE - 1:EE]))
        for k, hot in enumerate((r_h1, r_h2)):
            idx = (r_i1, r_i2)[k]
            then(dve.tensor_tensor(r_t, hot, r_rank, ALU.mult))
            then(dve.tensor_reduce(r_rk, r_t, AX.X, ALU.add))
            then(dve.tensor_tensor(r_t, hot, r_ov[:, 3, :].unsqueeze(1).broadcast_to([P, T, EE]), ALU.mult))
            then(dve.tensor_reduce(r_bs, r_t, AX.X, ALU.add))
            then(dve.tensor_tensor(r_c10, bc(r_rk, NTH - 1), th.unsqueeze(1).broadcast_to([P, T, NTH - 1]), ALU.is_ge))
            then(dve.tensor_reduce(r_c, r_c10, AX.X, ALU.add))
            then(dve.tensor_scalar(r_s, r_c, -float(CAP), None, ALU.mult))
            then(dve.tensor_tensor(r_s, r_s, r_rk, ALU.add))
            then(dve.tensor_scalar(r_z, r_c, 0.0, None, ALU.is_equal))
            then(dve.tensor_tensor(r_bs, r_bs, r_c, ALU.add))
            then(dve.tensor_scalar(r_bs, r_bs, float(NE - 1), None, ALU.add))
            then(dve.tensor_tensor(r_x, idx, r_bs, ALU.subtract))
            then(dve.tensor_tensor(r_x, r_x, r_z, ALU.mult))
            then(dve.tensor_tensor(r_bs, r_bs, r_x, ALU.add))
            then(dve.scalar_tensor_tensor(r_x, r_s, float(NBLK), r_bs, ALU.mult, ALU.add))
            then(dve.tensor_copy(pos_i[:, TILES * k:TILES * k + TILES], r_x))
            dve.tensor_copy(small_i[:, 1:2], small_i[:, 0:1]).then_inc(S("pos_done"), 1)
        dve.wait_ge(S("r_exp"), 2)
        then(dve.tensor_reduce(r_gw, r_ge, AX.X, ALU.add))
        then(dve.tensor_scalar(r_x, r_e2, 1.0, None, ALU.add))
        then(dve.tensor_tensor(r_gw, r_gw, r_x, ALU.mult))
        then(dve.reciprocal(w12[:, 0, :], r_gw))
        then(dve.tensor_tensor(w12[:, 1, :], w12[:, 0, :], r_e2, ALU.mult))
        dve.tensor_copy(small_i[:, 2:3], small_i[:, 0:1]).then_inc(S("routed"), 1)

        def take_rows(n, u):
            if not (isinstance(n, int) and n < 2):
                dve.wait_ge(S("gu_full"), n - 1)
            for j in range(2):
                dve.wait_ge(S("rowsT_full"), 2 * n + j + 1)
                dve.tensor_copy(xgT[u][:, 4 * j:4 * j + 4, :], bk[j][:, 0:4 * CAP].rearrange("p (g n) -> p g n", g=4)
                                ).then_inc(S("rowsT_done"), 1)

        def hidden(n, u):
            dve.wait_ge(S("silu"), n + 1)
            gbank = bk[2 + u][:, 0:4 * CAP].rearrange("p (s j n) -> p s j n", s=2, j=2)
            dve.tensor_tensor(hT[u], gbank[:, 1], sg[u], ALU.mult).then_inc(S("hidden"), 1)

        def experts(first, count):
            take_rows(first, 0)
            with dve.Fori(first // 2, (first + count) // 2 - 1) as i:
                take_rows(2 * i + 1, 1)
                hidden(2 * i, 0)
                take_rows(2 * i + 2, 0)
                hidden(2 * i + 1, 1)
            take_rows(first + count - 1, 1)
            hidden(first + count - 2, 0)
            hidden(first + count - 1, 1)

        experts(0, NE)
        over = dve.value_load(small_i[0:1, 0:1], min_val=0, max_val=NOV)
        with dve.If(over > 0):
            experts(NE, NOV)
        dve.end_ifs()

        def combine(a):
            n, u = a.rows, a.u
            dve.wait_ge(S(f"in{u}"), 32 * (a.k + 1) + 32 * USES[u])
            if not a.early:
                dve.wait_ge(S("out_done"), a.t - 1)
            dve.scalar_tensor_tensor(h2[u][0:n, :], y0[u][0:n, :], w12[0:n, 0, bass.ds(a.t, 1)], h[0:n, a.t, :],
                                     ALU.mult, ALU.add).then_inc(S("scaled"), 1)
            dve.wait_ge(S("scaled"), a.t + T + 1)
            dve.scalar_tensor_tensor(h2[u][0:n, :], y1[u][0:n, :], w12[0:n, 1, bass.ds(a.t, 1)], h2[u][0:n, :],
                                     ALU.mult, ALU.add).then_inc(S("h2_done"), 1)
            dve.wait_ge(S("ms"), a.t + 2 * T + 1)
            dve.reciprocal(rsf[0:n, u:u + 1], msf[0:n, u:u + 1]).then_inc(S("rstd"), 1)
            dve.wait_ge(S("rstd"), a.t + 2 * T + 1)
            dve.scalar_tensor_tensor(hn[u][0:n, :], h2[u][0:n, :], rsf[0:n, u:u + 1], gple[0:n, :],
                                     ALU.mult, ALU.mult).then_inc(S("hn_done"), 1)

        def finish(a):
            n, u = a.rows, a.u
            if not a.early:
                dve.wait_ge(S(f"out{u}"), 16 * (a.k + 2 * USES[u]))
            for j in range(2):
                c = slice(512 * j, 512 * j + 512)
                dve.wait_ge(S("pp_full"), 2 * a.t + j + 1)
                dve.wait_ge(S("gate_done"), 2 * a.t + j + 1)
                dve.tensor_tensor(ot[u][0:n, c], bk[4 + j][0:n, :], gs[u][0:n, c], ALU.mult).then_inc(S("ple_done"), 1)
            dve.wait_ge(S("ple_done"), 2 * a.t + 2)
            dve.tensor_tensor(ot[u][0:n, :], ot[u][0:n, :], h2[u][0:n, :], ALU.add).then_inc(S("out_done"), 1)

        def step_h(prev, cur, nxt):
            if nxt is not None:
                combine(nxt)
            finish(cur)

        dve.wait_ge(S("gple_in"), 16)
        combine(fixed(0))
        over_tiles(dve, step_h)

    @block.tensor
    def _(pe):
        mm = pe.matmul

        pe.wait_ge(S("const_in"), 16 * NCONST)
        pe.wait_ge(S("relbd_in"), 16 * 5)
        for j in range(3):
            mm(bk[4 + j][0:H, 0:384], relp, hotp[:, 384 * j:384 * j + 384], start=True, stop=True).then_inc(S("bias_full"), 1)
        mm(bk[2], relbd, hots[:, 0:512], start=True, stop=True).then_inc(S("bias_full"), 1)
        mm(bk[3][:, 0:SK + 2 * SAMP - 512], relbd, hots[:, 512:SK + 2 * SAMP], start=True, stop=True).then_inc(S("bias_full"), 1)
        for q in range(CC):
            last = pe.transpose(bk[7][:, 16 * q:16 * q + 16], st_in[:, P * q:P * q + P], ident[0:16, 0:16])
        last.then_inc(S("bias_full"), 1)

        def trans_x(a):
            n = a.rows
            pe.wait_ge(S("xn"), a.t + 1)
            if not a.first:
                pe.wait_ge(S("xT_done"), 2 * a.t)
            for j in range(2):
                for c in range(4 * j, 4 * j + 4):
                    last = pe.transpose(bk[j][:, P * (c % 4):P * (c % 4) + n], x_in[a.u][0:n, c:D:DC], ident[0:n, 0:n])
                last.then_inc(S("xT_full"), 1)
            
        def project(a, part):
            n = a.rows
            if part == 0:
                pe.wait_ge(S("xT_done"), 2 * a.t + 2)
            if a.first:
                pe.wait_ge(S(f"wA_in{part}"), 16)
            else:
                pe.wait_ge(S("prj_free"), 3 * a.t + part - 2)
            for c in range(DC):
                last = mm(bk[4 + part][0:n, :], xTs[a.u][:, c, 0:n], wA[:, c, AD * part:AD * part + AD],
                          start=(c == 0), stop=(c == DC - 1))
            last.then_inc(S("prj_full"), 1)

        def trans_qk(a):
            n = a.rows
            pe.wait_ge(S("qk_norm"), a.t + 1)
            if not a.first:
                pe.wait_ge(S("qkT_free"), a.t)
            for g in range(NG):
                last = pe.transpose(bk[2][:, P * g:P * g + n], qk[a.u][0:n, P * g:P * g + P], ident[0:n, 0:n])
            last.then_inc(S("qkT_full"), 1)
            if not a.first:
                pe.wait_ge(S("qkT_done"), a.t)
            for g in range(NG):
                last = pe.transpose(bk[3][:, P * g:P * g + n], qk[a.u][0:n, AD + P * g:AD + P * g + P], ident[0:n, 0:n])
            last.then_inc(S("qkT_full"), 1)

        pe.wait_ge(S("bias_done"), 7)
        trans_x(fixed(0))

        def step(prev, cur, nxt):
            project(cur, 0)
            project(cur, 1)
            if nxt is not None:
                trans_x(nxt)
            project(cur, 2)
            if prev is not None:
                trans_qk(prev)

        over_tiles(pe, step)

        pe.wait_ge(S("ones_set"), 3)
        pe.wait_ge(S("xT_kept"), TILES)
        pe.wait_ge(S("xT_done"), 2 * TILES)
        for q in range(CC):
            pe.wait_ge(S(f"wB_in{q % 2}"), 16 * (q // 2 + 1))
            for j, (lo, n) in enumerate(((0, 512), (512, 512), (SEQ, SAMP))):
                use = 3 * q + j
                for which, full, b in ((2, "cC_full", use % 2), (0, "ch_full", 2 + use % 2), (1, "cB_full", 4 + j)):
                    if which == 2 and use >= 2:
                        pe.wait_ge(S("cC_done"), use - 1)
                    if which == 0 and use >= 2:
                        pe.wait_ge(S("u_done"), use - 1)
                    if which == 1 and q >= 1:
                        pe.wait_ge(S("y_done"), 3 * (q - 1) + j + 1)
                    if which == 0 and use == 0:
                        trans_qk(fixed(8))
                        pe.wait_ge(S("qkT_done"), TILES)
                        pe.wait_ge(S("prj_free"), 3 * TILES)
                    for c in range(DC):
                        last = mm(bk[b][:, 0:n], wB[q % 2][:, c, which, :], xT[:, c, lo:lo + n], start=(c == 0), stop=(c == DC - 1))
                    last.then_inc(S(full), 1)
        pe.wait_ge(S("unew"), 2 * CC)
        pe.wait_ge(S("cC_done"), 3 * CC)
        for q in range(CC):
            last = pe.transpose(bk[0][0:18, P * q:P * q + P], u_new[:, 18 * q:18 * q + 18], ident[:, :])
        last.then_inc(S("new_full"), 1)
        pe.wait_ge(S("y_sum"), CC)
        for t in range(TILES):
            n = P if t < PT else SAMP
            last = mm(bk[7][0:n, t:t + 1], y_sum[:, P * t:P * t + n], ones[:, 0:1], start=True, stop=True)
        last.then_inc(S("ssc_full"), 1)
        pe.wait_ge(S("new_done"), 1)
        pe.wait_ge(S("ssc"), 3)
        pe.wait_ge(S("u_done"), 3 * CC)
        pe.wait_ge(S("y_done"), 3 * CC)

        with pe.Fori(0, 2) as it:
            for pp in range(2):
                base = 32 * it + 16 * pp
                t_use = [0]

                def score(n):
                    hh, i = ORDER[n]
                    lo, w = 64 * hh, P * (i + 1)
                    if n == 0:
                        pe.wait_ge(S("qst"), 6 * it + 3 * pp + 3)
                    pe.wait_ge(S("scored"), base + (n - 1 if n >= 2 else 0))
                    for c0 in range(0, w, 512):
                        m = min(512, w - c0)
                        last = mm(bank[n % 2][:, c0:c0 + m], qst[pp][lo:lo + 64, P * i:P * i + P],
                                  kst[pp][lo:lo + 64, c0:c0 + m], start=True, stop=True)
                    last.then_inc(S("s_full"), 1)

                def trans_p(n):
                    hh, i = ORDER[n]
                    pe.wait_ge(S("exp_done"), base + n + 1)
                    for j0 in range(0, i + 1, 4):
                        m = min(4, i + 1 - j0)
                        if t_use[0] >= 2:
                            pe.wait_ge(S("tp_free"), 48 * it + 24 * pp + t_use[0] - 1)
                        else:
                            pe.wait_ge(S("tp_free"), 48 * it + 24 * pp)
                        for j in range(m):
                            last = pe.transpose(bk[4 + t_use[0] % 2][:, P * j:P * j + P], Eb[n % 2][:, P * (j0 + j):P * (j0 + j) + P], ident[:, :])
                        last.then_inc(S("tp_full"), 1)
                        t_use[0] += 1
                    return t_use[0]

                def weigh(n, uses):
                    hh, i = ORDER[n]
                    pe.wait_ge(S("tp_free"), 48 * it + 24 * pp + uses)
                    pe.wait_ge(S("ot_copied"), base + n)
                    for j in range(i + 1):
                        last = mm(bk[6][0:DH + 1, 0:P], vst[pp][:, j, hh, :], PTb[n % 2][:, j, :],
                                  start=(j == 0), stop=(j == i))
                    last.then_inc(S("ot_full"), 1)

                def turn_o(n):
                    pe.wait_ge(S("ot_copied"), base + n + 1)
                    pe.wait_ge(S("o_free"), base + n)
                    pe.transpose(bk[7][:, 0:DH + 1], OT[n % 2], ident[0:DH + 1, 0:DH + 1]).then_inc(S("o_full"), 1)

                score(0)
                score(1)
                for n in range(16):
                    uses = trans_p(n)
                    if n + 2 < 16:
                        score(n + 2)
                    if n >= 1:
                        weigh(n - 1, last_uses)
                    if n >= 2:
                        turn_o(n - 2)
                    last_uses = uses
                weigh(15, last_uses)
                turn_o(14)
                turn_o(15)

        pe.wait_ge(S("o_free"), 64)
        with pe.Fori(0, 2) as g:
            for bb in range(4):
                pe.wait_ge(S(f"att_in{bb}"), 32 + 64 * g + 32)
                for gg in range(NG):
                    pe.wait_ge(S("kn_free"), 16 * g + 4 * bb + gg - 1) if (4 * bb + gg) >= 2 else pe.wait_ge(S("st_done"), 3 * g)
                    for r in range(4):
                        last = pe.transpose(bk[2 + gg % 2][:, P * r:P * r + P], KV[bb][:, 0, r, P * gg:P * gg + P], ident[:, :])
                    last.then_inc(S("kn_full"), 1)
                    if 4 * bb + gg >= 2:
                        pe.wait_ge(S("kf_free"), 16 * g + 4 * bb + gg - 1)
                    for r in range(NT):
                        last = pe.transpose(bk[4 + gg % 2][:, FAR * r:FAR * r + FAR], KV[bb][0:FAR, 1, r, P * gg:P * gg + P], ident[0:FAR, 0:FAR])
                    last.then_inc(S("kf_full"), 1)
                pe.wait_ge(S("kn_free"), 16 * g + 4 * bb + 4)
                pe.wait_ge(S("kf_free"), 16 * g + 4 * bb + 4)
                pe.wait_ge(S("qbd"), 10 * g + 10)
                pe.wait_ge(S("ss_scored"), g)
                rows = slice(32 * bb, 32 * bb + 32)
                for gg in range(NG):
                    mm(bk[0][rows, :], qbd[:, bb, gg, :, :].rearrange("p t h -> p (t h)"), ktc[:, gg, 0:NEAR],
                       start=(gg == 0), stop=(gg == NG - 1))
                for gg in range(NG):
                    last = mm(bk[1][rows, 0:SK - NEAR], qbd[:, bb, gg, :, :].rearrange("p t h -> p (t h)"), ktc[:, gg, NEAR:SK],
                              start=(gg == 0), stop=(gg == NG - 1))
                for gg in range(NG):
                    last = mm(bk[1][rows, SK - NEAR:SKN - NEAR], qbd[:, bb, gg, :, :].rearrange("p t h -> p (t h)"), kts[:, gg, :],
                              start=(gg == 0), stop=(gg == NG - 1))
                last.then_inc(S("ss_done"), 1)
            pe.wait_ge(S("ss_exp"), g + 1)
            for r in range(4):
                last = pe.transpose(bk[2][:, P * r:P * r + P], Es[:, P * r:P * r + P], ident[:, :])
            last.then_inc(S("st_full"), 1)
            for r in range(4):
                last = pe.transpose(bk[3][0:FAR, P * r:P * r + P], Es[:, NEAR + FAR * r:NEAR + FAR * r + FAR], ident[:, :])
            last.then_inc(S("st_full"), 1)
            pe.transpose(bk[4][0:SAMP, 0:P], Es[:, SK:SKN], ident[:, :]).then_inc(S("st_full"), 1)
            pe.wait_ge(S("st_done"), 3 * g + 3)
            pe.wait_ge(S("masked"), g)
            for bb in range(4):
                pe.wait_ge(S(f"att_in{bb}"), 32 + 64 * g + 64)
                rows = slice(32 * bb, 32 * bb + 32)
                for r in range(4):
                    mm(bk[6][rows, :], PTs[:, r, rows], KV[bb][:, 0, r, :], start=(r == 0), stop=False)
                for r in range(NT):
                    mm(bk[6][rows, :], PTs[0:FAR, 4 + r, rows], KV[bb][0:FAR, 1, r, :], start=False, stop=False)
                last = mm(bk[6][rows, :].rearrange("p (h d) -> p h d", h=H), PTs[0:SAMP, 8, rows], V[0:SAMP, PT, :, 0:DH], start=False, stop=True)
                last.then_inc(S("so_full"), 1)
            pe.wait_ge(S("masked"), g + 1)
            pe.wait_ge(S("sample_done"), g)
            mm(bk[7][0:SAMP, :], sel_st, masked, start=True, stop=True).then_inc(S("sum_full"), 1)

        def trans_att(a):
            n = a.rows
            pe.wait_ge(S("at_copied"), a.t + 1)
            if not a.first:
                pe.wait_ge(S("atT_done"), a.t)
            for q in range(CC):
                last = pe.transpose(bk[4][:, P * q:P * q + n], at_st[a.u][0:n, P * q:P * q + P], ident[0:n, 0:n])
            last.then_inc(S("atT_full"), 1)

        def out_att(a):
            n = a.rows
            pe.wait_ge(S("atT_done"), a.t + 1)
            for j in range(2):
                if not a.first:
                    pe.wait_ge(S("hA_done"), 2 * a.t + j - 1)
                for q in range(CC):
                    last = mm(bk[j][0:n, :], atT[a.u][:, q, 0:n], w_out[:, q, 512 * j:512 * j + 512], start=(q == 0), stop=(q == CC - 1))
                last.then_inc(S("oA_full"), 1)

        def out_conv(a):
            n = a.rows
            pe.wait_ge(S("y_copied"), a.t + 1)
            for j in range(2):
                if not a.first:
                    pe.wait_ge(S("h_done"), 2 * a.t + j - 1)
                for q in range(CC):
                    last = mm(bk[2 + j][0:n, :], y_st[a.u][:, q, 0:n], w_out[:, CC + q, 512 * j:512 * j + 512], start=(q == 0), stop=(q == CC - 1))
                last.then_inc(S("oC_full"), 1)

        def router(a):
            n = a.rows
            pe.wait_ge(S("m_done"), a.t + 1)
            for j in range(2):
                for c in range(4 * j, 4 * j + 4):
                    last = pe.transpose(bk[5 + j][:, P * (c % 4):P * (c % 4) + n], m_st[a.u][0:n, c:D:DC], ident[0:n, 0:n])
                last.then_inc(S("xT_full"), 1)

        def logits(a):
            n = a.rows
            pe.wait_ge(S("mT_done"), 2 * a.t + 2)
            if not a.first:
                pe.wait_ge(S("logits_done"), a.t)
            for c in range(DC):
                last = mm(bk[7][0:n, 0:RG], mT[a.u][:, c, 0:n], w_rt[:, c, :], start=(c == 0), stop=(c == DC - 1))
            last.then_inc(S("lg_full"), 1)

        def step_e(prev, cur, nxt):
            out_att(cur)
            if nxt is not None:
                trans_att(nxt)
            if prev is not None:
                router(prev)
            out_conv(cur)
            if prev is not None:
                logits(prev)

        pe.wait_ge(S("wout_in"), 16 * (2 * CC + 3))
        pe.wait_ge(S("sample_done"), 2)
        pe.wait_ge(S("ssc"), 5)
        trans_att(fixed(0))
        over_tiles(pe, step_e)
        router(fixed(8))
        logits(fixed(8))

        pe.wait_ge(S("r_sum"), 1)
        av = r_a.rearrange("p t e -> p (t e)")
        mm(bk[0][:, 0:TILES * NE], ones[:, :], av, start=True, stop=True).then_inc(S("rank_full"), 1)
        mm(bk[1][:, 0:TILES * NE], tri[:, :], av, start=True, stop=True).then_inc(S("rank_full"), 1)
        pe.wait_ge(S("routed"), 1)

        def trans_rows(n, u, k):
            pe.wait_ge(S(f"rows_in{u}"), 16 * (k + 1))
            for j in range(2):
                for c in range(4 * j, 4 * j + 4):
                    last = pe.transpose(bk[j][:, CAP * (c % 4):CAP * (c % 4) + CAP], xg[u][:, c:D:DC], ident[0:CAP, 0:CAP])
                last.then_inc(S("rowsT_full"), 1)

        def up(n, u, s, k4):
            pe.wait_ge(S("rowsT_done"), 2 * n + 2)
            pe.wait_ge(S(f"w_in{s}"), 48 * (k4 + 1))
            for w, side in ((wg[s], 0), (wu[s], 1)):
                for j in range(2):
                    for c in range(DC):
                        last = mm(bk[2 + u][:, CAP * (2 * side + j):CAP * (2 * side + j) + CAP], w[:, c, j:FE:2], xgT[u][:, c, :],
                                  start=(c == 0), stop=(c == DC - 1))
            last.then_inc(S("gu_full"), 1)

        def down(n, u, s):
            pe.wait_ge(S("hidden"), n + 1)
            for j in range(2):
                if not (isinstance(n, int) and n < 2):
                    pe.wait_ge(S("rows_done"), 2 * n - 3 + j)
                for q in range(2):
                    last = mm(bk[4 + 2 * u + j][0:CAP, :], hT[u][:, q, :], wd[s][:, q, 512 * j:512 * j + 512], start=(q == 0), stop=(q == 1))
                last.then_inc(S("y_full"), 1)

        def turn(i, s, begin=False, final=False):
            n = 4 * i + s
            up(n, s % 2, s, i)
            if not final:
                trans_rows(n + 1, 1 - s % 2, 2 * i + (s + 1) // 2)
            if not begin:
                down(n - 1, 1 - s % 2, (s - 1) % 4)
            if final:
                down(n, s % 2, s)

        for s in range(4):
            if s == 0:
                trans_rows(0, 0, 0)
            turn(0, s, begin=(s == 0))
        with pe.Fori(1, NE // 4 - 1) as i:
            for s in range(4):
                turn(i, s)
        for s in range(4):
            turn(NE // 4 - 1, s, final=(s == 3))
        over = pe.value_load(small_i[0:1, 0:1], min_val=0, max_val=NOV)
        with pe.If(over > 0):
            trans_rows(NE, 0, NE // 2)
            for s in range(4):
                turn(NE // 4, s, begin=(s == 0))
            with pe.Fori(NE // 4 + 1, NBLK // 4 - 1) as i:
                for s in range(4):
                    turn(i, s)
            for s in range(4):
                turn(NBLK // 4 - 1, s, final=(s == 3))
            pe.wait_ge(S("rows_done"), 2 * NBLK)
        pe.end_ifs()

        def trans_p(a):
            n = a.rows
            pe.wait_ge(S(f"p_in{a.u}"), 16 * (a.k + 1))
            if not a.first:
                pe.wait_ge(S("pT_done"), a.t)
            for q in range(2):
                last = pe.transpose(bk[6][:, P * q:P * q + n], p_in[a.u][0:n, q:PLE:2], ident[0:n, 0:n])
            last.then_inc(S("pT_full"), 1)

        def trans_h(a):
            n = a.rows
            pe.wait_ge(S("hn_done"), a.t + 1)
            for j in range(2):
                if not a.first:
                    pe.wait_ge(S("mT_done"), 2 * (a.t + T) + j - 1)
                for c in range(4 * j, 4 * j + 4):
                    last = pe.transpose(bk[j][:, P * (c % 4):P * (c % 4) + n], hn[a.u][0:n, c:D:DC], ident[0:n, 0:n])
                last.then_inc(S("xT_full"), 1)

        def embed(a):
            n = a.rows
            pe.wait_ge(S("pT_done"), a.t + 1)
            for j in range(2):
                if not a.first:
                    pe.wait_ge(S("ple_done"), 2 * a.t + j - 1)
                for q in range(2):
                    last = mm(bk[4 + j][0:n, :], pT[a.u][:, q, 0:n], w_pp[:, q, 512 * j:512 * j + 512], start=(q == 0), stop=(q == 1))
                last.then_inc(S("pp_full"), 1)

        def gates(a):
            n = a.rows
            pe.wait_ge(S("mT_done"), 2 * (a.t + T) + 2)
            for j in range(2):
                if not a.first:
                    pe.wait_ge(S("gate_done"), 2 * a.t + j - 1)
                for c in range(DC):
                    last = mm(bk[2 + j][0:n, :], hnT[a.u][:, c, 0:n], w_pg[c][:, 512 * j:512 * j + 512], start=(c == 0), stop=(c == DC - 1))
                last.then_inc(S("gate_full"), 1)

        def step_h(prev, cur, nxt):
            if prev is not None:
                embed(cur)
            gates(cur)
            if nxt is not None:
                trans_p(nxt)
                trans_h(nxt)

        pe.wait_ge(S("rows_done"), 2 * NE)
        trans_p(fixed(0))
        pe.wait_ge(S("wpp_in"), 32)
        embed(fixed(0))
        trans_h(fixed(0))
        pe.wait_ge(S("wpg_in"), 16 * DC)
        over_tiles(pe, step_h)


OUTS = [(1, SEQ, D), (NB, NT, D), (1, 1, SEQ, H, DH), (1, 1, SEQ, H, DH), (1, 1, 2, CD),
        (1, NB, NT, H, DH), (1, NB, NT, H, DH), (1, NB, 2, CD)]


def kernel(**inputs):
    import concourse.bacc as bacc
    from concourse.bass_utils import run_bass_kernel_spmd as run

    nc = bacc.Bacc("TRN2", target_bir_lowering=False, num_devices=1)
    arrays, I = {}, {}
    for name, a in list(inputs.items()) + list(constants().items()):
        a = np.ascontiguousarray(a)
        arrays[f"in_{name}"] = a
        I[name] = nc.dram_tensor(f"in_{name}", a.shape, mybir.dt.from_np(a.dtype), kind="ExternalInput").ap()
    full = [nc.dram_tensor(f"out_{i}", shape, F32, kind="ExternalOutput").ap() for i, shape in enumerate(OUTS)]
    O = [full[0][0], full[1].rearrange("b t d -> (b t) d"),
         full[2][0, 0].rearrange("s h d -> s (h d)"), full[3][0, 0].rearrange("s h d -> s (h d)"), full[4][0, 0],
         full[5][0].rearrange("b t h d -> (b t) (h d)"), full[6][0].rearrange("b t h d -> (b t) (h d)"),
         full[7][0].rearrange("b j c -> (b j) c")]
    build(nc, I, O)
    r = run(nc, [arrays], core_ids=[0])
    return tuple(r.results[0][f"out_{i}"] for i in range(len(OUTS)))
```
